# Optimizing a Trainium2 kernel written in Bass

```python
import jax, jax.numpy as jnp
from jax import lax
import numpy as np

'''
One inference step of a hybrid chunk-causal streaming encoder (DEPTH post-norm layers), run for two
request groups that share every weight.
Layer:  h1 = LN1(alpha*h + W_out(sig(gA) * P_A(DSA(h)) + sig(gB) * P_B(GLA(h))))
        h2 = LN2(alpha*h1 + PEER(h1))
DSA  = indexer-selected sparse grouped-query softmax attention with rotary positions (gathered top-k keys).
GLA  = gated linear attention (per-token causal, evaluated in chunks of CHUNK frames).
PEER = product-key retrieval over P_EXPERTS single-neuron experts.
Inputs:
  x_prompt    (BATCH, SEQ, D_MODEL)            first chunks, positions 0..SEQ-1
  x_sample    (DEC_BATCH, DEC_SEQ, D_MODEL)    later chunk, positions PAST_LEN..PAST_LEN+DEC_SEQ-1
  cache_k     (DEPTH, DEC_BATCH, PAST_LEN, A_KV_HEADS, A_HEAD_DIM)  rotary-applied keys
  cache_v     (DEPTH, DEC_BATCH, PAST_LEN, A_KV_HEADS, A_HEAD_DIM)  values
  cache_idx_k (DEPTH, DEC_BATCH, PAST_LEN, IDX_DIM)                 rotary-applied indexer keys
  state_gla   (DEPTH, DEC_BATCH, G_HEADS, G_KEY_DIM, G_VAL_DIM)     GLA recurrent state
  then the weights (leading DEPTH axis).
Returns (y_prompt, y_sample, k_prompt, v_prompt, idx_k_prompt, gla_prompt,
         k_sample, v_sample, idx_k_sample, gla_sample):
  y_prompt (BATCH, SEQ, D_MODEL), y_sample (DEC_BATCH, DEC_SEQ, D_MODEL)
  k_prompt, v_prompt (DEPTH, BATCH, SEQ, A_KV_HEADS, A_HEAD_DIM), idx_k_prompt (DEPTH, BATCH, SEQ, IDX_DIM)
  gla_prompt (DEPTH, BATCH, G_HEADS, G_KEY_DIM, G_VAL_DIM)
  k_sample, v_sample (DEPTH, DEC_BATCH, DEC_SEQ, A_KV_HEADS, A_HEAD_DIM), idx_k_sample (DEPTH, DEC_BATCH, DEC_SEQ, IDX_DIM)
  gla_sample (DEPTH, DEC_BATCH, G_HEADS, G_KEY_DIM, G_VAL_DIM)
'''

D_MODEL = 1024
BATCH = 1
SEQ = 1024
DEPTH = 1
DEC_BATCH = 1
DEC_SEQ = 32
PAST_LEN = 512

CHUNK = 64
A_HEADS = 8
A_KV_HEADS = 2
A_HEAD_DIM = 64
A_GROUP = A_HEADS // A_KV_HEADS
IDX_HEADS = 4
IDX_DIM = 64
IDX_TOPK = 256
Q_BLOCK = 128
ROPE_THETA = 10000.0
G_HEADS = 4
G_KEY_DIM = 128
G_VAL_DIM = 128
G_LOWRANK = 16
G_TAU = 16.0
P_HEADS = 8
P_NKEYS = 128
P_EXPERTS = P_NKEYS * P_NKEYS
P_QDIM = 256
P_HALF = P_QDIM // 2
P_TOPK = 16
P_BLOCK = 128
DN_ALPHA = (2.0 * DEPTH) ** 0.25
DN_BETA = (8.0 * DEPTH) ** -0.25
LN_EPS = 1e-5

W_AQ = A_HEADS * A_HEAD_DIM
W_AK = A_KV_HEADS * A_HEAD_DIM
W_AV = A_KV_HEADS * A_HEAD_DIM
W_IQ = IDX_HEADS * IDX_DIM
W_IK = IDX_DIM
W_IW = IDX_HEADS
W_GQ = G_HEADS * G_KEY_DIM
W_GK = G_HEADS * G_KEY_DIM
W_GV = G_HEADS * G_VAL_DIM
W_GF = G_LOWRANK
W_GR = G_HEADS * G_VAL_DIM
W_GATE = 2 * D_MODEL
IN_SIZES = (W_AQ, W_AK, W_AV, W_IQ, W_IK, W_IW, W_GQ, W_GK, W_GV, W_GF, W_GR, W_GATE)
IN_COLS = sum(IN_SIZES)

kernel_name = 'dsa_gla_peer_streaming_step'

def layer_norm(x, g, b):
    xf = x.astype(jnp.float32)
    mu = jnp.mean(xf, -1, keepdims=True)
    var = jnp.mean(jnp.square(xf - mu), -1, keepdims=True)
    return ((xf - mu) * lax.rsqrt(var + LN_EPS) * g + b).astype(x.dtype)

def rope(x, pos):
    half = x.shape[-1] // 2
    inv = ROPE_THETA ** (-jnp.arange(half, dtype=jnp.float32) / half)
    ang = pos.astype(jnp.float32)[:, None] * inv[None, :]
    cos = jnp.cos(ang)[None, :, None, :]
    sin = jnp.sin(ang)[None, :, None, :]
    x1 = x[..., :half].astype(jnp.float32)
    x2 = x[..., half:].astype(jnp.float32)
    return jnp.concatenate([x1 * cos - x2 * sin, x2 * cos + x1 * sin], -1).astype(x.dtype)

def mixer_inputs(h, pos, w_in, w_fa, b_fa):
    B, T = h.shape[0], h.shape[1]
    cuts = np.cumsum(IN_SIZES)[:-1].tolist()
    aq, ak, av, iq, ik, iw, gq, gk, gv, gf, gr, gate = jnp.split(h @ w_in, cuts, axis=-1)
    aq = rope(aq.reshape(B, T, A_HEADS, A_HEAD_DIM), pos)
    ak = rope(ak.reshape(B, T, A_KV_HEADS, A_HEAD_DIM), pos)
    av = av.reshape(B, T, A_KV_HEADS, A_HEAD_DIM)
    iq = rope(iq.reshape(B, T, IDX_HEADS, IDX_DIM), pos)
    ik = rope(ik.reshape(B, T, 1, IDX_DIM), pos)[:, :, 0]
    gq = gq.reshape(B, T, G_HEADS, G_KEY_DIM) * (G_KEY_DIM ** -0.5)
    gk = gk.reshape(B, T, G_HEADS, G_KEY_DIM)
    gv = gv.reshape(B, T, G_HEADS, G_VAL_DIM)
    glog = (jax.nn.log_sigmoid((gf @ w_fa + b_fa).astype(jnp.float32)) / G_TAU).reshape(B, T, G_HEADS, G_KEY_DIM)
    gate_a, gate_b = jnp.split(gate, 2, axis=-1)
    return aq, ak, av, iq, ik, iw, gq, gk, gv, glog, gr, gate_a, gate_b

def sparse_attention(aq, iq, iw, k_all, v_all, ik_all, limit):
    B, Tq = aq.shape[0], aq.shape[1]
    L = k_all.shape[1]
    topk = min(IDX_TOPK, L // 4)
    s = jnp.einsum('bqhd,bsd->bqhs', iq.astype(jnp.float32), ik_all.astype(jnp.float32)) * (IDX_DIM ** -0.5)
    score = jnp.einsum('bqhs,bqh->bqs', jax.nn.relu(s), iw.astype(jnp.float32) * (IDX_HEADS ** -0.5))
    admissible = jnp.arange(L)[None, :] < limit[:, None]
    score = jnp.where(admissible[None], score, -jnp.inf)
    sel_score, sel = lax.top_k(score, topk)
    valid = jnp.isfinite(sel_score)
    gather = jax.vmap(lambda t, i: t[i])
    kg = gather(k_all, sel)
    vg = gather(v_all, sel)
    q = aq.reshape(B, Tq, A_KV_HEADS, A_GROUP, A_HEAD_DIM).astype(jnp.float32)
    logits = jnp.einsum('bqngd,bqknd->bqngk', q, kg.astype(jnp.float32)) * (A_HEAD_DIM ** -0.5)
    logits = jnp.where(valid[:, :, None, None, :], logits, -jnp.inf)
    p = jax.nn.softmax(logits, axis=-1)
    o = jnp.einsum('bqngk,bqknd->bqngd', p, vg.astype(jnp.float32))
    return o.reshape(B, Tq, A_HEADS * A_HEAD_DIM).astype(aq.dtype)

def prompt_sparse_attention(aq, iq, iw, ak, av, ik):
    B, T = aq.shape[0], aq.shape[1]
    nb = T // Q_BLOCK
    def blocks(a):
        return jnp.moveaxis(a.reshape((B, nb, Q_BLOCK) + a.shape[2:]), 1, 0)
    limit = ((jnp.arange(T) // CHUNK) + 1) * CHUNK
    def one(args):
        q_b, iq_b, iw_b, lim_b = args
        return sparse_attention(q_b, iq_b, iw_b, ak, av, ik, lim_b)
    o = lax.map(one, (blocks(aq), blocks(iq), blocks(iw), limit.reshape(nb, Q_BLOCK)))
    return jnp.moveaxis(o, 0, 1).reshape(B, T, A_HEADS * A_HEAD_DIM)

def gla_chunk(state, q, k, v, g):
    C = q.shape[1]
    b = jnp.cumsum(g, axis=1)
    causal = jnp.tril(jnp.ones((C, C), dtype=bool))
    diff = b[:, :, None] - b[:, None, :]
    decay = jnp.exp(jnp.where(causal[None, :, :, None, None], diff, -jnp.inf))
    qf = q.astype(jnp.float32)
    kf = k.astype(jnp.float32)
    vf = v.astype(jnp.float32)
    attn = jnp.einsum('bthc,bshc,btshc->bhts', qf, kf, decay)
    o = jnp.einsum('bhts,bshv->bthv', attn, vf) + jnp.einsum('bthc,bhcv->bthv', qf * jnp.exp(b), state)
    b_last = b[:, -1]
    new_state = jnp.exp(b_last)[..., None] * state + jnp.einsum('bshc,bshv->bhcv', kf * jnp.exp(b_last[:, None] - b), vf)
    return new_state, o

def gla_prompt(q, k, v, g):
    B, T = q.shape[0], q.shape[1]
    nc = T // CHUNK
    def chunks(a):
        return jnp.moveaxis(a.reshape((B, nc, CHUNK) + a.shape[2:]), 1, 0)
    s0 = jnp.zeros((B, G_HEADS, G_KEY_DIM, G_VAL_DIM), jnp.float32)
    s_final, o = lax.scan(lambda s, xs: gla_chunk(s, xs[0], xs[1], xs[2], xs[3]), s0,
                          (chunks(q), chunks(k), chunks(v), chunks(g)))
    return s_final, jnp.moveaxis(o, 0, 1).reshape(B, T, G_HEADS, G_VAL_DIM)

def branch_merge(h, o_attn, o_gla, gr, gate_a, gate_b, g_norm, w_pa, w_pb, w_out):
    B, T = h.shape[0], h.shape[1]
    of = o_gla.astype(jnp.float32)
    of = of * lax.rsqrt(jnp.mean(jnp.square(of), -1, keepdims=True) + LN_EPS) * g_norm.reshape(G_HEADS, G_VAL_DIM)
    o_b = (of.reshape(B, T, G_HEADS * G_VAL_DIM) * jax.nn.silu(gr.astype(jnp.float32))).astype(h.dtype)
    ya = o_attn @ w_pa
    yb = o_b @ w_pb
    m = jax.nn.sigmoid(gate_a) * ya + jax.nn.sigmoid(gate_b) * yb
    return m @ w_out

def peer(h, w_pq, pk1, pk2, pu, pv):
    n = h.shape[0]
    q = (h @ w_pq).reshape(n, P_HEADS, 2, P_HALF).astype(jnp.float32)
    s1 = jnp.einsum('nhd,hkd->nhk', q[:, :, 0], pk1.astype(jnp.float32))
    s2 = jnp.einsum('nhd,hkd->nhk', q[:, :, 1], pk2.astype(jnp.float32))
    v1, i1 = lax.top_k(s1, P_TOPK)
    v2, i2 = lax.top_k(s2, P_TOPK)
    cand = (v1[..., :, None] + v2[..., None, :]).reshape(n, P_HEADS, P_TOPK * P_TOPK)
    cidx = (i1[..., :, None] * P_NKEYS + i2[..., None, :]).reshape(n, P_HEADS, P_TOPK * P_TOPK)
    sc, j = lax.top_k(cand, P_TOPK)
    e = jnp.take_along_axis(cidx, j, axis=-1)
    g = jax.nn.softmax(sc, axis=-1)
    ue = pu[e]
    ve = pv[e]
    a = jax.nn.gelu(jnp.einsum('nhkd,nd->nhk', ue, h).astype(jnp.float32), approximate=False)
    return jnp.einsum('nhk,nhkd->nd', (g * a).astype(h.dtype), ve)

def peer_blocked(h, w_pq, pk1, pk2, pu, pv):
    B, T, D = h.shape
    flat = h.reshape(-1, P_BLOCK, D)
    out = lax.map(lambda hb: peer(hb, w_pq, pk1, pk2, pu, pv), flat)
    return out.reshape(B, T, D)

def setup_inputs(seed: int = 0) -> dict:
    key = jax.random.key(seed)
    ks = jax.random.split(key, 24)
    def nrm(k, shape, scale):
        return jax.random.normal(k, shape, jnp.float32) * scale
    col_scale = jnp.concatenate([jnp.full((n,), DN_BETA if i in (2, 8) else 1.0, jnp.float32)
                                 for i, n in enumerate(IN_SIZES)])
    return {
        'x_prompt': nrm(ks[0], (BATCH, SEQ, D_MODEL), 1.0),
        'x_sample': nrm(ks[1], (DEC_BATCH, DEC_SEQ, D_MODEL), 1.0),
        'cache_k': nrm(ks[2], (DEPTH, DEC_BATCH, PAST_LEN, A_KV_HEADS, A_HEAD_DIM), 1.0),
        'cache_v': nrm(ks[3], (DEPTH, DEC_BATCH, PAST_LEN, A_KV_HEADS, A_HEAD_DIM), DN_BETA),
        'cache_idx_k': nrm(ks[4], (DEPTH, DEC_BATCH, PAST_LEN, IDX_DIM), 1.0),
        'state_gla': nrm(ks[5], (DEPTH, DEC_BATCH, G_HEADS, G_KEY_DIM, G_VAL_DIM), 1.0),
        'w_in': nrm(ks[6], (DEPTH, D_MODEL, IN_COLS), D_MODEL ** -0.5) * col_scale,
        'w_fa': nrm(ks[7], (DEPTH, G_LOWRANK, G_HEADS * G_KEY_DIM), G_LOWRANK ** -0.5),
        'b_fa': nrm(ks[8], (DEPTH, G_HEADS * G_KEY_DIM), 0.1),
        'g_gla_norm': 1.0 + nrm(ks[9], (DEPTH, G_HEADS * G_VAL_DIM), 0.02),
        'w_pa': nrm(ks[10], (DEPTH, A_HEADS * A_HEAD_DIM, D_MODEL), (A_HEADS * A_HEAD_DIM) ** -0.5 * DN_BETA),
        'w_pb': nrm(ks[11], (DEPTH, G_HEADS * G_VAL_DIM, D_MODEL), (G_HEADS * G_VAL_DIM) ** -0.5 * DN_BETA),
        'w_out': nrm(ks[12], (DEPTH, D_MODEL, D_MODEL), D_MODEL ** -0.5 * DN_BETA),
        'ln1_g': 1.0 + nrm(ks[13], (DEPTH, D_MODEL), 0.02),
        'ln1_b': nrm(ks[14], (DEPTH, D_MODEL), 0.02),
        'w_pq': nrm(ks[15], (DEPTH, D_MODEL, P_HEADS * P_QDIM), D_MODEL ** -0.5),
        'pk1': nrm(ks[16], (DEPTH, P_HEADS, P_NKEYS, P_HALF), P_HALF ** -0.5),
        'pk2': nrm(ks[17], (DEPTH, P_HEADS, P_NKEYS, P_HALF), P_HALF ** -0.5),
        'pu': nrm(ks[18], (DEPTH, P_EXPERTS, D_MODEL), D_MODEL ** -0.5),
        'pv': nrm(ks[19], (DEPTH, P_EXPERTS, D_MODEL), DN_BETA),
        'ln2_g': 1.0 + nrm(ks[20], (DEPTH, D_MODEL), 0.02),
        'ln2_b': nrm(ks[21], (DEPTH, D_MODEL), 0.02),
    }

def reference(x_prompt, x_sample, cache_k, cache_v, cache_idx_k, state_gla, w_in, w_fa, b_fa, g_gla_norm,
              w_pa, w_pb, w_out, ln1_g, ln1_b, w_pq, pk1, pk2, pu, pv, ln2_g, ln2_b):
    Tp = x_prompt.shape[1]
    Ts = x_sample.shape[1]
    P = cache_k.shape[2]
    pos_p = jnp.arange(Tp)
    pos_s = P + jnp.arange(Ts)
    lim_s = jnp.full((Ts,), P + Ts, jnp.int32)
    hp = x_prompt
    hs = x_sample
    kp_l, vp_l, ikp_l, sp_l = [], [], [], []
    ks_l, vs_l, iks_l, ss_l = [], [], [], []
    for l in range(DEPTH):
        aq, ak, av, iq, ik, iw, gq, gk, gv, glog, gr, ga, gb = mixer_inputs(hp, pos_p, w_in[l], w_fa[l], b_fa[l])
        o_a = prompt_sparse_attention(aq, iq, iw, ak, av, ik)
        s_fin, o_b = gla_prompt(gq, gk, gv, glog)
        mix = branch_merge(hp, o_a, o_b, gr, ga, gb, g_gla_norm[l], w_pa[l], w_pb[l], w_out[l])
        hp = layer_norm(DN_ALPHA * hp + mix, ln1_g[l], ln1_b[l])
        hp = layer_norm(DN_ALPHA * hp + peer_blocked(hp, w_pq[l], pk1[l], pk2[l], pu[l], pv[l]), ln2_g[l], ln2_b[l])
        kp_l.append(ak)
        vp_l.append(av)
        ikp_l.append(ik)
        sp_l.append(s_fin.astype(x_prompt.dtype))
        aq, ak, av, iq, ik, iw, gq, gk, gv, glog, gr, ga, gb = mixer_inputs(hs, pos_s, w_in[l], w_fa[l], b_fa[l])
        k_all = jnp.concatenate([cache_k[l], ak], axis=1)
        v_all = jnp.concatenate([cache_v[l], av], axis=1)
        ik_all = jnp.concatenate([cache_idx_k[l], ik], axis=1)
        o_a = sparse_attention(aq, iq, iw, k_all, v_all, ik_all, lim_s)
        s_new, o_b = gla_chunk(state_gla[l].astype(jnp.float32), gq, gk, gv, glog)
        mix = branch_merge(hs, o_a, o_b, gr, ga, gb, g_gla_norm[l], w_pa[l], w_pb[l], w_out[l])
        hs = layer_norm(DN_ALPHA * hs + mix, ln1_g[l], ln1_b[l])
        hs_flat = hs.reshape(-1, D_MODEL)
        hs = layer_norm(DN_ALPHA * hs + peer(hs_flat, w_pq[l], pk1[l], pk2[l], pu[l], pv[l]).reshape(hs.shape),
                        ln2_g[l], ln2_b[l])
        ks_l.append(ak)
        vs_l.append(av)
        iks_l.append(ik)
        ss_l.append(s_new.astype(x_sample.dtype))
    return (hp, hs, jnp.stack(kp_l), jnp.stack(vp_l), jnp.stack(ikp_l), jnp.stack(sp_l),
            jnp.stack(ks_l), jnp.stack(vs_l), jnp.stack(iks_l), jnp.stack(ss_l))


_drawn_inputs = setup_inputs


def setup_inputs(seed=0):
    import zlib

    import numpy as np

    out = dict(_drawn_inputs(seed))
    spreads = {}
    factors = {'g_gla_norm': 5.0, 'ln2_g': 2.939, 'ln2_b': 2.749}
    for name, (base, spread) in spreads.items():
        noise = np.random.default_rng([zlib.crc32(name.encode()), seed]).standard_normal(out[name].shape)
        drawn = base * np.exp(spread * noise) if base else spread * noise
        out[name] = __import__('jax').numpy.asarray(drawn.astype(out[name].dtype))
    for name, factor in factors.items():
        out[name] = (out[name] * factor).astype(out[name].dtype)
    return out
```

```python
from contextlib import ExitStack

import concourse.bass as bass
from concourse import mybir

F32 = mybir.dt.float32
U32 = mybir.dt.uint32
ALU = mybir.AluOpType
ACT = mybir.ActivationFunctionType
AX = mybir.AxisListType

P = 128
D = 1024
KD = D // P
TP = 1024
TS = 32
PAST = 512
NT = TP + TS
TILES = TP // P + 1
SAMPLE = TILES - 1
ROWS = [P] * (TILES - 1) + [TS]
CHUNK = 64
HEADS, KV, HD, GROUP = 8, 2, 64, 4
IH, ID = 4, 64
TOPK_P = min(256, TP // 4)
TOPK_S = min(256, (PAST + TS) // 4)
GH, GK = 4, 128
GC = 32
NCH = NT // GC
TAU = 16.0
LOWRANK = 16
PH, NKEYS, PK = 8, 128, 16
NEXP = NKEYS * NKEYS
EPS = 1e-5
ALPHA = 2.0 ** 0.25
C_AV, C_IQ, C_IW, C_GQ, C_GK, C_GV, C_GF, C_GR, C_GATE = 640, 768, 1088, 1092, 1604, 2116, 2628, 2644, 3156
DSA = C_GQ
GONE = -3.0e38
STAIR = [PK // (i + 1) for i in range(PK)]
STAIR_AT = [sum(STAIR[:i]) for i in range(PK)]
NCAND = sum(STAIR)


def stair_runs():
    runs, i = [], 0
    while i < PK:
        n = sum(1 for k in STAIR[i:] if k == STAIR[i])
        runs.append((i, n, STAIR[i], STAIR_AT[i]))
        i += n
    return runs


def tok(t):
    return slice(t * P, t * P + ROWS[t])


class Link:

    def __init__(self, eng, sem):
        self.eng, self.sem, self.n = eng, sem, 0

    def add(self, ins):
        self.n += 1
        ins.then_inc(self.sem, 1)

    def wait(self):
        if self.n:
            self.eng.wait_ge(self.sem, self.n)


def project_attention(nc, io, res, sem):
    with ExitStack() as ctx:
        def sb(name, shape):
            return ctx.enter_context(nc.sbuf_tensor(name, shape, F32))
        w = sb("w_dsa", [P, KD, DSA])
        z = sb("z", [P, 2, DSA])
        ta = sb("rope_a", [P, 960])
        tb = sb("rope_b", [P, 960])
        rot = sb("rot", [P, 2, 1024])
        cos = sb("cos_sb", [P, TILES, HD])
        sin = sb("sin_sb", [P, TILES, HD])
        zps = ctx.enter_context(nc.psum_tensor("zps", [P, 2, 3 * 512], F32))
        tps = ctx.enter_context(nc.psum_tensor("tps", [P, 1024], F32))
        ident, xT = res["ident"], res["xT"]
        consts_in, w_in_, sample_in = sem("consts_in"), sem("w_dsa_in"), sem("sample_in")
        z_ready, z_copied, rope_step, rot_ready = sem("z_ready"), sem("z_copied"), sem("rope_step"), sem("rot_ready")
        turned, turned_copied, kv_out = sem("turned"), sem("turned_copied"), [sem("kv_out0"), sem("kv_out1")]
        bounds = [(0, 512), (512, 1024), (1024, DSA)]

        with nc.Block() as block:
            @block.sync
            def _(sp):
                for dst, src in ((cos[:], io["cos"]), (sin[:], io["sin"])):
                    sp.dma_start(dst, src).then_inc(consts_in, 16)
                wv = io["w_in"].rearrange("(k p) n -> p k n", p=P)
                for a, b in bounds:
                    sp.dma_start(w[:, :, a:b], wv[:, :, a:b]).then_inc(w_in_, 16)
                sp.dma_start(res["kTs"][:, 0:PAST], io["kcT"]).then_inc(sample_in, 16)
                sp.dma_start(res["ikTs"][:, 0:PAST], io["ikcT"]).then_inc(sample_in, 16)
                sp.dma_start(res["Vs"][:, 0:PAST // P, :], io["vc"].rearrange("(c p) n -> p c n", p=P)).then_inc(sample_in, 16)
                for t in range(TILES):
                    R = ROWS[t]
                    k_o, v_o, ik_o = (io["k_p"], io["v_p"], io["ik_p"]) if t < SAMPLE else (io["k_s"], io["v_s"], io["ik_s"])
                    row = slice(t * P, t * P + R) if t < SAMPLE else slice(0, R)
                    sp.wait_ge(rot_ready, t + 1)
                    sp.wait_ge(z_copied, t + 1)
                    v_src = res["V"][:, t, :] if t < SAMPLE else res["Vs"][0:R, PAST // P, :]
                    sp.dma_start(k_o[row, :], rot[0:R, t % 2, 512:640]).then_inc(kv_out[t % 2], 16)
                    sp.dma_start(ik_o[row, :], rot[0:R, t % 2, 896:960]).then_inc(kv_out[t % 2], 16)
                    sp.dma_start(v_o[row, :], v_src).then_inc(kv_out[t % 2], 16)
                for b in range(2):
                    sp.wait_ge(kv_out[b], 48 * len(range(b, TILES, 2)))
                sp.wait_ge(sample_in, 48)

            @block.tensor
            def _(pe):
                def transposes(t):
                    R = ROWS[t]
                    pe.wait_ge(rot_ready, t + 1)
                    if t:
                        pe.wait_ge(turned_copied, t)
                    for b in range(8):
                        last = pe.transpose(tps[:, b * P:b * P + R], rot[0:R, t % 2, b * P:(b + 1) * P], ident[0:R, 0:R])
                    last.then_inc(turned, 1)

                pe.wait_ge(w_in_, 48)
                for t in range(TILES):
                    if t >= 2:
                        pe.wait_ge(z_copied, t - 1)
                    for c, (a, b) in enumerate(bounds):
                        for k in range(KD):
                            last = pe.matmul(zps[0:ROWS[t], t % 2, c * 512:c * 512 + b - a], xT[:, k, tok(t)], w[:, k, a:b],
                                             start=(k == 0), stop=(k == KD - 1))
                    last.then_inc(z_ready, 1)
                    if t >= 1:
                        transposes(t - 1)
                transposes(SAMPLE)

            @block.scalar
            def _(act):
                def copies(t):
                    R = ROWS[t]
                    act.wait_ge(turned, t + 1)
                    tv = tps[:].rearrange("p (b r) -> p b r", b=8)[:, :, 0:R]
                    s = tok(t)
                    act.copy(res["aqT"][:, :, s], tv[:, 0:4, :])
                    act.copy(res["iqT"][:, :, s], tv[:, 5:7, :])
                    kT, ikT, at = (res["kT"], res["ikT"], t * P) if t < SAMPLE else (res["kTs"], res["ikTs"], PAST)
                    act.copy(kT[:, at:at + R], tv[:, 4, :])
                    act.copy(ikT[:, at:at + R], tv[:, 7, :]).then_inc(turned_copied, 1)

                for t in range(TILES):
                    R = ROWS[t]
                    act.wait_ge(z_ready, t + 1)
                    if t >= 2:
                        act.wait_ge(rot_ready, t - 1)
                    act.copy(z[0:R, t % 2, :], zps[0:R, t % 2, 0:DSA])
                    v_dst = res["V"][:, t, :] if t < SAMPLE else res["Vs"][0:R, PAST // P, :]
                    act.copy(v_dst, zps[0:R, t % 2, C_AV:C_IQ])
                    act.mul(res["iw"][0:R, t, :], zps[0:R, t % 2, C_IW:DSA], IH ** -0.5 * ID ** -0.5).then_inc(z_copied, 1)
                    if t >= 1:
                        copies(t - 1)
                copies(SAMPLE)

            @block.vector
            def _(dve):
                link = Link(dve, rope_step)
                dve.wait_ge(consts_in, 32)
                for t in range(TILES):
                    R, b = ROWS[t], t % 2
                    dve.wait_ge(z_copied, t + 1)
                    if t >= 1:
                        dve.wait_ge(rot_ready, t)
                    for z0, n, o in ((0, 10, 0), (C_IQ, 5, 640)):
                        zv = z[0:R, b, z0:z0 + n * HD].rearrange("p (h d) -> p h d", d=HD)
                        av = ta[0:R, o:o + n * HD].rearrange("p (h d) -> p h d", d=HD)
                        bv = tb[0:R, o:o + n * HD].rearrange("p (h d) -> p h d", d=HD)
                        cv = cos[0:R, t:t + 1, :].to_broadcast([R, n, HD])
                        dve.tensor_tensor(av, zv, cv, ALU.mult)
                        for lo, hi in ((0, 32), (32, 0)):
                            sv = sin[0:R, t:t + 1, lo:lo + 32].to_broadcast([R, n, 32])
                            last = dve.tensor_tensor(bv[:, :, lo:lo + 32], zv[:, :, hi:hi + 32], sv, ALU.mult)
                    link.add(last)
                    link.wait()
                    if t >= 2:
                        dve.wait_ge(turned, t - 1)
                        dve.wait_ge(kv_out[b], 48 * (t // 2))
                    dve.tensor_tensor(rot[0:R, b, 0:512].rearrange("p (g n d) -> p n g d", g=GROUP, n=KV),
                                      ta[0:R, 0:512].rearrange("p (n g d) -> p n g d", g=GROUP, n=KV),
                                      tb[0:R, 0:512].rearrange("p (n g d) -> p n g d", g=GROUP, n=KV), ALU.add)
                    dve.tensor_tensor(rot[0:R, b, 512:960], ta[0:R, 512:960], tb[0:R, 512:960], ALU.add)
                    dve.tensor_tensor(rot[0:R, b, 960:1024], ta[0:R, 896:960], tb[0:R, 896:960], ALU.add).then_inc(rot_ready, 1)


def gated_linear(nc, io, res, sem):
    MID = GC // 2 - 1
    with ExitStack() as ctx:
        def sb(name, shape):
            return ctx.enter_context(nc.sbuf_tensor(name, shape, F32))
        wk = sb("w_gk", [P, 2, 2, KD, P])
        wvr = sb("w_gvr", [P, KD, 512])
        wgf = sb("w_gf", [P, KD, LOWRANK])
        wfa = sb("w_fa_sb", [LOWRANK, GH * GK])
        bfa = sb("b_fa_sb", [P, GH])
        gnorm = sb("gnorm", [P, GH * GK])
        mask = sb("gla_mask_sb", [P, P])
        reset = sb("reset_sb", [P, NT])
        gfT = sb("gfT", [LOWRANK, NT])
        gv = sb("gv", [P, TILES, GH * GK])
        og = sb("og", [P, TILES, GH * GK])
        spare = res["late"][:, 0:4 * NT].rearrange("p (x n) -> p x n", x=4)
        q, k = spare[:, 0, :], spare[:, 1, :]
        f = [sb(f"gla_f{i}", [P, NT])[:] for i in range(4)] + [spare[:, 2, :], spare[:, 3, :]]
        dec = sb("dec", [P, NCH])
        at = sb("gla_at", [P, 2, P])
        kl = sb("gla_kl", [P, 2, P])
        S = sb("gla_S", [P, 8, P])
        S0 = sb("gla_S0", [P, GH, P])
        gsil = sb("gsil", [P, 2, GH * GK])
        sq = sb("sq", [P, P])
        ss = sb("ss", [P, TILES, GH])
        pp = ctx.enter_context(nc.psum_tensor("gla_pp", [P, 3, 512], F32))
        pa = ctx.enter_context(nc.psum_tensor("gla_pa", [P, 2, 512], F32))
        po = ctx.enter_context(nc.psum_tensor("gla_po", [P, 512], F32))
        pu = ctx.enter_context(nc.psum_tensor("gla_pu", [P, 2, 512], F32))
        ident, xT = res["ident"], res["xT"]
        g_in = sem("gla_in")
        v_in, r_in = sem("w_gv_in"), sem("w_gr_in")
        wk_in = [sem("w_gk_in0"), sem("w_gk_in1")]
        gf_ready, gf_copied, gv_ready, gv_copied = sem("gf_ready"), sem("gf_copied"), sem("gv_ready"), sem("gv_copied")
        pre_ready, pre_used, q_ready, q_copied, k_ready, k_copied = (sem(n) for n in
            ("pre_ready", "pre_used", "gq_ready", "gq_copied", "gk_ready", "gk_copied"))
        soft_step, gates, scan_done, gdiff, gexp, dve_step, factors = (sem(n) for n in
            ("soft_step", "gla_gates", "scan_done", "gdiff", "gexp", "gla_step", "gla_factors"))
        at_ready, at_masked, kl_ready, kl_copied, u_ready, s_next, o_ready, o_copied = (sem(n) for n in
            ("at_ready", "at_masked", "kl_ready", "kl_copied", "u_ready", "s_next", "o_ready", "o_copied"))
        s_out, gr_ready, gr_sig, gr_done, ob_step, ob_ready, obt_ready, obt_copied, s0_in = (sem(n) for n in
            ("s_out", "gr_ready", "gr_sig", "gr_done", "ob_step", "ob_ready", "obt_ready", "obt_copied", "s0_in"))
        ss_ready, ss_root, u_part = sem("ss_ready"), sem("ss_root"), sem("u_part")
        TC = [(0, 352), (352, 704), (704, 1056)]
        NJ = [r // GC for r in ROWS]

        with nc.Block() as block:
            @block.sync
            def _(sp):
                wv = io["w_in"].rearrange("(k p) n -> p k n", p=P)
                for dst, src in ((wgf[:], wv[:, :, C_GF:C_GR]), (wfa[:], io["w_fa"]), (bfa[:], io["b_fa"]),
                                 (gnorm[:], io["g_gla_norm"].to_broadcast([P, GH * GK])),
                                 (mask[:], io["gla_mask"]), (reset[:], io["reset"]),
                                 (S0[:], io["state"].rearrange("h c v -> c h v"))):
                    sp.dma_start(dst, src).then_inc(g_in, 16)
                sp.dma_start(wvr[:], wv[:, :, C_GV:C_GF]).then_inc(v_in, 16)
                for h in range(GH):
                    if h >= 2:
                        sp.wait_ge(k_ready, h - 1)
                    sp.dma_start(wk[:, h % 2, 0, :, :], wv[:, :, C_GQ + h * P:C_GQ + (h + 1) * P]).then_inc(wk_in[h % 2], 16)
                    sp.dma_start(wk[:, h % 2, 1, :, :], wv[:, :, C_GK + h * P:C_GK + (h + 1) * P]).then_inc(wk_in[h % 2], 16)
                sp.wait_ge(gv_ready, TILES)
                sp.dma_start(wvr[:], wv[:, :, C_GR:C_GATE]).then_inc(r_in, 16)

            @block.gpsimd
            def _(pool):
                for h in range(GH):
                    pool.wait_ge(s_next, h * NCH + NCH - 1)
                    pool.dma_start(io["gla_p"][h], S[:, (NCH - 1) % 8, :]).then_inc(s_out, 16)
                    pool.wait_ge(s_next, h * NCH + NCH)
                    pool.dma_start(io["gla_s"][h], S[:, NCH % 8, :]).then_inc(s_out, 16)
                    pool.wait_ge(s_out, 32 * (h + 1))

            @block.tensor
            def _(pe):
                pe.wait_ge(g_in, 7 * 16)
                for c, (a, b) in enumerate(TC):
                    for kk in range(KD):
                        last = pe.matmul(pp[0:LOWRANK, c, 0:b - a], wgf[:, kk, :], xT[:, kk, a:b], start=(kk == 0), stop=(kk == KD - 1))
                last.then_inc(gf_ready, 1)
                pe.wait_ge(v_in, 16)
                for t in range(TILES):
                    if t >= 2:
                        pe.wait_ge(gv_copied, t - 1)
                    for kk in range(KD):
                        last = pe.matmul(pa[0:ROWS[t], t % 2, :], xT[:, kk, tok(t)], wvr[:, kk, :], start=(kk == 0), stop=(kk == KD - 1))
                    last.then_inc(gv_ready, 1)
                pe.wait_ge(gf_copied, 1)
                for h in range(GH):
                    if h:
                        pe.wait_ge(k_copied, h)
                    for c, (a, b) in enumerate(TC):
                        last = pe.matmul(pp[:, c, 0:b - a], wfa[:, h * P:(h + 1) * P], gfT[:, a:b], start=True, stop=True)
                    last.then_inc(pre_ready, 1)
                    pe.wait_ge(wk_in[h % 2], 32 * (h // 2 + 1))
                    pe.wait_ge(pre_used, h + 1)
                    pe.wait_ge(soft_step, 3 * h + 1)
                    for c, (a, b) in enumerate(TC):
                        for kk in range(KD):
                            last = pe.matmul(pp[:, c, 0:b - a], wk[:, h % 2, 0, kk, :], xT[:, kk, a:b], start=(kk == 0), stop=(kk == KD - 1))
                    last.then_inc(q_ready, 1)
                    pe.wait_ge(q_copied, h + 1)
                    for c, (a, b) in enumerate(TC):
                        for kk in range(KD):
                            last = pe.matmul(pp[:, c, 0:b - a], wk[:, h % 2, 1, kk, :], xT[:, kk, a:b], start=(kk == 0), stop=(kk == KD - 1))
                    last.then_inc(k_ready, 1)
                    pe.wait_ge(k_copied, h + 1)
                    pe.wait_ge(factors, h + 1)
                    pe.wait_ge(gv_copied, TILES)
                    for t in range(TILES):
                        n, R = h * TILES + t, ROWS[t]
                        s = tok(t)
                        if n >= 1:
                            pe.wait_ge(at_masked, n)
                            pe.wait_ge(kl_copied, n)
                        pe.matmul(pa[0:R, 0, 0:R], f[1][:, s], f[0][:, s], start=True, stop=True).then_inc(at_ready, 1)
                        pe.transpose(pa[0:R, 1, 0:P], f[3][:, s], ident[:]).then_inc(kl_ready, 1)
                        pe.wait_ge(kl_copied, n + 1)
                        if n >= 2:
                            m = n - 2
                            pe.wait_ge(s_next, (m // TILES) * NCH + sum(NJ[:m % TILES + 1]))
                        for j in range(NJ[t]):
                            if j:
                                pe.wait_ge(u_part, h * 3 * SAMPLE + 3 * t + j)
                            last = pe.matmul(pu[:, n % 2, j * P:(j + 1) * P], kl[GC * j:GC * (j + 1), n % 2, :],
                                             gv[GC * j:GC * (j + 1), t, h * P:(h + 1) * P], start=True, stop=True)
                            last.then_inc(u_part if j < NJ[t] - 1 else u_ready, 1)
                        pe.wait_ge(at_masked, n + 1)
                        if n >= 1:
                            pe.wait_ge(o_copied, n)
                        pe.matmul(po[0:R, 0:P], at[0:R, n % 2, 0:R], gv[0:R, t, h * P:(h + 1) * P], start=True, stop=False)
                        for j in range(NJ[t]):
                            i = t * (P // GC) + j
                            if t < SAMPLE:
                                if i or h:
                                    pe.wait_ge(s_next, h * NCH + i)
                            st = S[:, i % 8, :] if t < SAMPLE else S0[:, h, :]
                            last = pe.matmul(po[GC * j:GC * (j + 1), 0:P], f[2][:, i * GC:(i + 1) * GC], st,
                                             start=False, stop=True)
                        last.then_inc(o_ready, 1)
                pe.wait_ge(r_in, 16)
                for t in range(TILES):
                    pe.wait_ge(at_masked, GH * TILES)
                    if t >= 2:
                        pe.wait_ge(gr_done, t - 1)
                    for kk in range(KD):
                        last = pe.matmul(pa[0:ROWS[t], t % 2, :], xT[:, kk, tok(t)], wvr[:, kk, :], start=(kk == 0), stop=(kk == KD - 1))
                    last.then_inc(gr_ready, 1)
                for t in range(TILES):
                    R = ROWS[t]
                    pe.wait_ge(ob_ready, t + 1)
                    if t >= 2:
                        pe.wait_ge(obt_copied, t - 1)
                    for b in range(4):
                        last = pe.transpose(pu[:, t % 2, b * P:b * P + R], og[0:R, t, b * P:(b + 1) * P], ident[0:R, 0:R])
                    last.then_inc(obt_ready, 1)

            @block.scalar
            def _(act):
                act.wait_ge(gf_ready, 1)
                for c, (a, b) in enumerate(TC):
                    last = act.copy(gfT[:, a:b], pp[0:LOWRANK, c, 0:b - a])
                last.then_inc(gf_copied, 1)
                for t in range(TILES):
                    act.wait_ge(gv_ready, t + 1)
                    act.copy(gv[0:ROWS[t], t, :], pa[0:ROWS[t], t % 2, :]).then_inc(gv_copied, 1)
                act.wait_ge(g_in, 7 * 16)

                def whole(x):
                    return x.rearrange("p (c n) -> p c n", c=3)
                for h in range(GH):
                    act.wait_ge(pre_ready, h + 1)
                    if h:
                        act.wait_ge(o_ready, h * TILES)
                    act.activation(whole(f[0]), pp[:, :, 0:352], ACT.Abs, bias=bfa[:, h:h + 1]).then_inc(soft_step, 1)
                    act.wait_ge(soft_step, 3 * h + 1)
                    act.activation(f[0], f[0], ACT.Exp, scale=-1.0).then_inc(soft_step, 1)
                    act.wait_ge(soft_step, 3 * h + 2)
                    act.activation(f[0], f[0], ACT.Ln, bias=1.0).then_inc(soft_step, 1)
                    act.wait_ge(q_ready, h + 1)
                    act.mul(whole(q), pp[:, :, 0:352], GK ** -0.5).then_inc(q_copied, 1)
                    act.wait_ge(k_ready, h + 1)
                    act.copy(whole(k), pp[:, :, 0:352]).then_inc(k_copied, 1)
                    act.wait_ge(gdiff, h + 1)
                    act.wait_ge(soft_step, 3 * h + 3)
                    act.activation(f[0], f[4], ACT.Exp, scale=1.0 / TAU)
                    act.activation(f[1], f[4], ACT.Exp, scale=-1.0 / TAU)
                    act.activation(f[2], f[5], ACT.Exp, scale=1.0 / TAU)
                    act.activation(f[3], f[3], ACT.Exp, scale=1.0 / TAU)
                    act.activation(dec[:].unsqueeze(2), f[5].rearrange("p (c n) -> p c n", n=GC)[:, :, GC - 1:GC],
                                   ACT.Exp, scale=1.0 / TAU).then_inc(gexp, 1)
                    for t in range(TILES):
                        n, R = h * TILES + t, ROWS[t]
                        act.wait_ge(kl_ready, n + 1)
                        if n >= 2:
                            act.wait_ge(u_ready, n - 1)
                        act.copy(kl[0:R, n % 2, :], pa[0:R, 1, 0:P]).then_inc(kl_copied, 1)
                        act.wait_ge(o_ready, n + 1)
                        act.copy(og[0:R, t, h * P:(h + 1) * P], po[0:R, 0:P]).then_inc(o_copied, 1)
                for t in range(TILES):
                    R = ROWS[t]
                    act.wait_ge(gr_ready, t + 1)
                    if t >= 2:
                        act.wait_ge(ob_ready, t - 1)
                    act.activation(gsil[0:R, t % 2, :], pa[0:R, t % 2, :], ACT.Sigmoid).then_inc(gr_sig, 1)
                    act.wait_ge(ss_ready, t + 1)
                    act.activation(ss[0:R, t, :], ss[0:R, t, :], ACT.Sqrt).then_inc(ss_root, 1)
                for t in range(TILES):
                    R = ROWS[t]
                    act.wait_ge(obt_ready, t + 1)
                    act.copy(res["obT"][:, :, tok(t)], pu[:, t % 2, :].rearrange("p (b r) -> p b r", b=4)[:, :, 0:R]).then_inc(obt_copied, 1)

            @block.vector
            def _(dve):
                link = Link(dve, dve_step)
                dve.wait_ge(g_in, 7 * 16)

                def chunks(x):
                    return x.rearrange("p (c n) -> p c n", n=GC)
                for h in range(GH):
                    dve.wait_ge(pre_ready, h + 1)
                    if h:
                        dve.wait_ge(o_ready, h * TILES)
                    link.wait()
                    dve.wait_ge(soft_step, 3 * h + 1)
                    dve.tensor_scalar(f[3].rearrange("p (c n) -> p c n", c=3), pp[:, :, 0:352], bfa[:, h:h + 1], 0.0,
                                      ALU.add, ALU.min).then_inc(pre_used, 1)
                    dve.wait_ge(pre_used, h + 1)
                    dve.wait_ge(soft_step, 3 * h + 3)
                    link.add(dve.tensor_tensor(f[4], f[3], f[0], ALU.subtract))
                    link.wait()
                    link.add(dve.tensor_tensor_scan(f[5], reset[:], f[4], 0.0, ALU.mult, ALU.add))
                    link.wait()
                    b3 = chunks(f[5])
                    dve.tensor_tensor(chunks(f[4]), b3, b3[:, :, MID:MID + 1].to_broadcast([P, NCH, GC]), ALU.subtract)
                    dve.tensor_tensor(chunks(f[3]), b3[:, :, GC - 1:GC].to_broadcast([P, NCH, GC]), b3, ALU.subtract).then_inc(gdiff, 1)
                    if h:
                        dve.wait_ge(s_out, 32 * h)
                        dve.wait_ge(s_next, h * NCH)
                    link.add(dve.memset(S[:, 0, :], 0.0))
                    dve.wait_ge(gexp, h + 1)
                    dve.wait_ge(q_copied, h + 1)
                    dve.wait_ge(k_copied, h + 1)
                    dve.tensor_tensor(f[0], f[0], q, ALU.mult)
                    dve.tensor_tensor(f[1], f[1], k, ALU.mult)
                    dve.tensor_tensor(f[2], f[2], q, ALU.mult)
                    dve.tensor_tensor(f[3], f[3], k, ALU.mult).then_inc(factors, 1)
                    link.wait()
                    for t in range(TILES):
                        n, R = h * TILES + t, ROWS[t]
                        dve.wait_ge(at_ready, n + 1)
                        if n >= 2:
                            dve.wait_ge(o_ready, n - 1)
                        dve.tensor_tensor(at[0:R, n % 2, 0:R], pa[0:R, 0, 0:R], mask[0:R, 0:R], ALU.mult).then_inc(at_masked, 1)
                        dve.wait_ge(u_ready, n + 1)
                        for j in range(NJ[t]):
                            i = t * (P // GC) + j
                            src = S[:, i % 8, :] if t < SAMPLE else S0[:, h, :]
                            if i or h:
                                dve.wait_ge(s_next, h * NCH + i)
                            dve.scalar_tensor_tensor(S[:, (i + 1) % 8, :], src, dec[:, i:i + 1], pu[:, n % 2, j * P:(j + 1) * P],
                                                     ALU.mult, ALU.add).then_inc(s_next, 1)
                for t in range(TILES):
                    R = ROWS[t]
                    dve.wait_ge(o_copied, GH * TILES)
                    for h in range(GH):
                        o = og[0:R, t, h * P:(h + 1) * P]
                        link.wait()
                        link.add(dve.tensor_tensor_reduce(sq[0:R, :], o, o, 1.0 / P, 0.0, ALU.mult, ALU.add, ss[0:R, t, h:h + 1]))
                    link.wait()
                    dve.tensor_scalar(ss[0:R, t, :], ss[0:R, t, :], EPS, None, ALU.add).then_inc(ss_ready, 1)
                    dve.wait_ge(gr_sig, t + 1)
                    link.add(dve.tensor_tensor(gsil[0:R, t % 2, :], gsil[0:R, t % 2, :], gnorm[0:R, :], ALU.mult))
                    link.wait()
                    dve.tensor_tensor(gsil[0:R, t % 2, :], gsil[0:R, t % 2, :], pa[0:R, t % 2, :], ALU.mult).then_inc(gr_done, 1)
                    dve.wait_ge(ss_root, t + 1)
                    link.add(dve.reciprocal(ss[0:R, t, :], ss[0:R, t, :]))
                    link.wait()
                    dve.wait_ge(gr_done, t + 1)
                    for h in range(GH):
                        o = og[0:R, t, h * P:(h + 1) * P]
                        last = dve.scalar_tensor_tensor(o, o, ss[0:R, t, h:h + 1], gsil[0:R, t % 2, h * P:(h + 1) * P], ALU.mult, ALU.mult)
                    last.then_inc(ob_ready, 1)


def sparse_attention(nc, io, res, sem):
    with ExitStack() as ctx:
        def sb(name, shape):
            return ctx.enter_context(nc.sbuf_tensor(name, shape, F32))
        rl = sb("relu", [P, 2, TP])
        score = sb("score", [P, 2, TP])
        bias = sb("bias", [P, 2, TP])
        m8 = sb("m8", [P, 2, 8])
        lg = sb("logits", [P, 2, TP])
        pr = sb("probs", [P, 2, TP])
        prT = sb("probsT", [P, 2, TP])
        mx = sb("mx", [P, HEADS])
        nmx = sb("nmx", [P, HEADS])
        sm = sb("sm", [P, 2, HEADS])
        rs = sb("rs", [P, HEADS])
        oa = sb("oa", [P, 2, 512])
        ps = ctx.enter_context(nc.psum_tensor("att_ps", [P, 2, TP], F32))
        pt = ctx.enter_context(nc.psum_tensor("att_pt", [P, TP], F32))
        po = ctx.enter_context(nc.psum_tensor("att_po", [P, 512], F32))
        px = ctx.enter_context(nc.psum_tensor("att_px", [P, 512], F32))
        ident = res["ident"]
        (is_ready, relu_done, sc_step, round_step, sel_ready, lg_ready, lg_done, mx_done, p_ready, pt_ready, pt_copied, o_ready,
         oa_step, oa_ready, oat_ready, oat_copied) = (sem(n) for n in (
            "is_ready", "relu_done", "sc_step", "round_step", "sel_ready", "lg_ready", "lg_done", "mx_done", "p_ready",
            "pt_ready", "pt_copied", "att_o_ready", "oa_step", "oa_ready", "oat_ready", "oat_copied"))
        LEN = [(t + 1) * P for t in range(SAMPLE)] + [PAST + TS]
        NEED = [TOPK_P] * SAMPLE + [TOPK_S]
        CHOOSE = [t for t in range(TILES) if LEN[t] > NEED[t]]

        def keys(t):
            return [(a, min(a + 512, LEN[t])) for a in range(0, LEN[t], 512)]

        def kchunks(t):
            return [(a, min(a + P, LEN[t])) for a in range(0, LEN[t], P)]

        order = [(t, kind, h) for t in range(TILES) for kind, nh in (("index", IH if t in CHOOSE else 0), ("logit", HEADS)) for h in range(nh)]
        slot = {key: n for n, key in enumerate(order)}

        def seen(key):
            return sum(1 for x in order[:slot[key] + 1] if x[1] == key[1])

        with nc.Block() as block:
            @block.tensor
            def _(pe):
                def free(n):
                    if n >= 2:
                        key = order[n - 2]
                        pe.wait_ge(relu_done if key[1] == "index" else lg_done, seen(key))

                def scores(t, kind, h):
                    n, R = slot[(t, kind, h)], ROWS[t]
                    free(n)
                    if kind == "index":
                        base, l, kT = HD * (h % 2), res["iqT"][:, h // 2, tok(t)], res["ikT"] if t < SAMPLE else res["ikTs"]
                    else:
                        base, l, kT = HD * (h // GROUP), res["aqT"][:, h % GROUP, tok(t)], res["kT"] if t < SAMPLE else res["kTs"]
                    for a, b in keys(t):
                        last = pe.matmul(ps[0:R, n % 2, a:b], l[base:base + HD, :], kT[base:base + HD, a:b], start=True, stop=True)
                    last.then_inc(is_ready if kind == "index" else lg_ready, 1)

                def values(t, h):
                    R, m = ROWS[t], t * HEADS + h
                    pe.wait_ge(p_ready, m + 1)
                    if m >= 1:
                        pe.wait_ge(pt_copied, m)
                    for c, (a, b) in enumerate(kchunks(t)):
                        last = pe.transpose(pt[0:b - a, c * P:c * P + R], pr[0:R, m % 2, a:b], ident[0:R, 0:R])
                    last.then_inc(pt_ready, 1)
                    pe.wait_ge(pt_copied, m + 1)
                    if h == 0 and t >= 1:
                        pe.wait_ge(oa_ready, t)
                    V = res["V"] if t < SAMPLE else res["Vs"]
                    ch = kchunks(t)
                    for c, (a, b) in enumerate(ch):
                        last = pe.matmul(po[0:R, h * HD:(h + 1) * HD], prT[0:b - a, m % 2, c * P:c * P + R],
                                         V[0:b - a, c, (h // GROUP) * HD:(h // GROUP + 1) * HD], start=(c == 0), stop=(c == len(ch) - 1))
                    last.then_inc(o_ready, 1)

                for t in range(TILES):
                    if t in CHOOSE:
                        for h in range(IH):
                            scores(t, "index", h)
                    for h in range(HEADS):
                        scores(t, "logit", h)
                        if h >= 1:
                            values(t, h - 1)
                    values(t, HEADS - 1)
                    R = ROWS[t]
                    pe.wait_ge(oa_ready, t + 1)
                    if t >= 1:
                        pe.wait_ge(oat_copied, t)
                    for b in range(4):
                        last = pe.transpose(px[:, b * P:b * P + R], oa[0:R, t % 2, b * P:(b + 1) * P], ident[0:R, 0:R])
                    last.then_inc(oat_ready, 1)

            @block.scalar
            def _(act):
                def probs(t, h):
                    R, m, L = ROWS[t], t * HEADS + h, LEN[t]
                    act.wait_ge(mx_done, m + 1)
                    if m >= 2:
                        act.wait_ge(pt_ready, m - 1)
                    act.activation(pr[0:R, m % 2, 0:L], lg[0:R, m % 2, 0:L], ACT.Exp, bias=nmx[0:R, h:h + 1], scale=HD ** -0.5,
                                   accum_out=sm[0:R, t % 2, h:h + 1]).then_inc(p_ready, 1)

                def turned(t, h):
                    R, m = ROWS[t], t * HEADS + h
                    act.wait_ge(pt_ready, m + 1)
                    if m >= 2:
                        act.wait_ge(o_ready, m - 1)
                    ch = kchunks(t)
                    full = [c for c, (a, b) in enumerate(ch) if b - a == P]
                    v = pt[:].rearrange("p (c r) -> p c r", r=P)
                    d = prT[:, m % 2, :].rearrange("p (c r) -> p c r", r=P)
                    last = act.copy(d[:, 0:len(full), 0:R], v[:, 0:len(full), 0:R])
                    if len(full) < len(ch):
                        k = ch[-1][1] - ch[-1][0]
                        last = act.copy(d[0:k, len(full), 0:R], v[0:k, len(full), 0:R])
                    last.then_inc(pt_copied, 1)

                nrelu = 0
                for t in range(TILES):
                    if t in CHOOSE:
                        for h in range(IH):
                            R, L = ROWS[t], LEN[t]
                            act.wait_ge(is_ready, nrelu + 1)
                            if nrelu >= 2:
                                act.wait_ge(sc_step, nrelu - 1)
                            act.activation(rl[0:R, nrelu % 2, 0:L], ps[0:R, slot[(t, "index", h)] % 2, 0:L], ACT.Relu).then_inc(relu_done, 1)
                            nrelu += 1
                    for h in range(HEADS):
                        probs(t, h)
                        if h >= 1:
                            turned(t, h - 1)
                    turned(t, HEADS - 1)
                    act.wait_ge(oat_ready, t + 1)
                    act.copy(res["oaT"][:, :, tok(t)], px[:].rearrange("p (b r) -> p b r", b=4)[:, :, 0:ROWS[t]]).then_inc(oat_copied, 1)

            @block.vector
            def _(dve):
                link = Link(dve, round_step)
                summed = 0

                def choose(t):
                    nonlocal summed
                    R, L = ROWS[t], LEN[t]
                    s = score[0:R, t % 2, :]
                    for h in range(IH):
                        dve.wait_ge(relu_done, summed + 1)
                        link.wait()
                        if h:
                            dve.wait_ge(sc_step, summed)
                        w = res["iw"][0:R, t, h:h + 1]
                        r = rl[0:R, summed % 2, 0:L]
                        if h == 0:
                            ins = dve.tensor_scalar(s[:, 0:L], r, w, None, ALU.mult)
                        else:
                            ins = dve.scalar_tensor_tensor(s[:, 0:L], r, w, s[:, 0:L], ALU.mult, ALU.add)
                        ins.then_inc(sc_step, 1)
                        summed += 1
                    dve.wait_ge(sc_step, summed)
                    if t < SAMPLE:
                        link.add(dve.memset(score[0:CHUNK, t % 2, L - CHUNK:L], GONE))
                        link.wait()
                    for r in range(NEED[t] // 8):
                        link.add(dve.max(m8[0:R, r % 2, :], s[:, 0:L]))
                        link.wait()
                        link.add(dve.match_replace(s[:, 0:L], m8[0:R, r % 2, :], s[:, 0:L], GONE))
                        link.wait()

                for t in range(TILES):
                    R, L = ROWS[t], LEN[t]
                    bv = bias[0:R, t % 2, :]
                    if t in CHOOSE:
                        choose(t)
                        link.add(dve.tensor_scalar(bv[:, 0:L], score[0:R, t % 2, 0:L], GONE, -1.0e30, ALU.is_gt, ALU.mult))
                    else:
                        link.add(dve.memset(bv[:, 0:L], 0.0))
                    link.wait()
                    if t < SAMPLE:
                        link.add(dve.memset(bias[0:CHUNK, t % 2, L - CHUNK:L], -1.0e30))
                        link.wait()
                    for h in range(HEADS):
                        m = t * HEADS + h
                        dve.wait_ge(lg_ready, m + 1)
                        if m >= 2:
                            dve.wait_ge(p_ready, m - 1)
                        dve.tensor_tensor_reduce(lg[0:R, m % 2, 0:L], ps[0:R, slot[(t, "logit", h)] % 2, 0:L], bv[:, 0:L], 1.0, -1.0e38,
                                                 ALU.add, ALU.max, mx[0:R, h:h + 1]).then_inc(lg_done, 1)
                        dve.wait_ge(lg_done, m + 1)
                        if t >= 1:
                            dve.wait_ge(p_ready, m - HEADS + 1)
                        dve.tensor_scalar(nmx[0:R, h:h + 1], mx[0:R, h:h + 1], -HD ** -0.5, None, ALU.mult).then_inc(mx_done, 1)
                    dve.wait_ge(p_ready, (t + 1) * HEADS)
                    dve.wait_ge(mx_done, (t + 1) * HEADS)
                    link.wait()
                    link.add(dve.reciprocal(rs[0:R, :], sm[0:R, t % 2, :]))
                    link.wait()
                    dve.wait_ge(o_ready, (t + 1) * HEADS)
                    if t >= 2:
                        dve.wait_ge(oat_ready, t - 1)
                    dve.tensor_tensor(oa[0:R, t % 2, :].rearrange("p (h d) -> p h d", d=HD), po[0:R, :].rearrange("p (h d) -> p h d", d=HD),
                                      rs[0:R, :].unsqueeze(2).to_broadcast([R, HEADS, HD]), ALU.mult).then_inc(oa_ready, 1)
                    dve.wait_ge(oa_ready, t + 1)


def layer_norm(dve, link, x, st, mv, gain, offset, R, root_asked, root_given, nth):
    for c in range(2):
        link.add(dve.bn_stats(st[0:R, c * 6:c * 6 + 6], x[:, c * 512:(c + 1) * 512]))
    link.wait()
    link.add(dve.bn_aggr(mv[0:R, 0:2], st[0:R, :]))
    link.wait()
    dve.tensor_scalar(mv[0:R, 1:2], mv[0:R, 1:2], EPS, None, ALU.add).then_inc(root_asked, 1)
    dve.wait_ge(root_given, nth + 1)
    link.add(dve.reciprocal(mv[0:R, 1:2], mv[0:R, 1:2]))
    link.wait()
    link.add(dve.tensor_scalar(x, x, mv[0:R, 0:1], mv[0:R, 1:2], ALU.subtract, ALU.mult))
    link.wait()
    link.add(dve.tensor_tensor(x, x, gain[0:R, :], ALU.mult))
    link.wait()
    return dve.tensor_tensor(x, x, offset[0:R, :], ALU.add)


def merge(nc, io, res, sem):
    with ExitStack() as ctx:
        def sb(name, shape):
            return ctx.enter_context(nc.sbuf_tensor(name, shape, F32))
        wb = sb("w_merge", [P, 2, 24, P])
        wo = sb("w_out_sb", [P, KD, D])
        mT = sb("mT", [P, KD, NT])
        sg = sb("sig", [P, 2, 2, 352])
        pr = sb("gated", [P, 2, 352])
        xt = sb("x_tok", [P, 2, D])
        gain, offset = sb("ln1_g_sb", [P, D]), sb("ln1_b_sb", [P, D])
        st, mv = sb("ln1_st", [P, 12]), sb("ln1_mv", [P, 2])
        pm = ctx.enter_context(nc.psum_tensor("mg_pm", [P, 8, 512], F32))
        ident, xT = res["ident"], res["xT"]
        (ln_in, wo_in, g_ready, sig_done, g_step, m_ready, mix_ready, mix_used, ln_step, root_asked,
         root_given, h_ready, ht_ready, ht_copied) = (sem(n) for n in (
            "ln1_in", "w_out_in", "g_ready", "sig_done", "g_step", "m_ready", "mix_ready", "mix_used",
            "ln1_step", "root1_asked", "root1_given", "h1_ready", "h1t_ready", "h1t_copied"))
        wb_in = [sem("w_merge_in0"), sem("w_merge_in1")]
        xt_in = [sem("x_tok_in0"), sem("x_tok_in1")]
        TC = [(0, 352), (352, 704), (704, 1056)]

        with nc.Block() as block:
            @block.sync
            def _(sp):
                wv = io["w_in"].rearrange("(k p) n -> p k n", p=P)
                pav = io["w_pa"].rearrange("(k p) n -> p k n", p=P)
                pbv = io["w_pb"].rearrange("(k p) n -> p k n", p=P)
                for f in range(KD):
                    if f >= 2:
                        sp.wait_ge(g_ready, 3 * (f - 1))
                    for lo, n, src, c in ((0, 8, wv, C_GATE), (8, 8, wv, C_GATE + D), (16, 4, pav, 0), (20, 4, pbv, 0)):
                        sp.dma_start(wb[:, f % 2, lo:lo + n, :], src[:, :, c + f * P:c + (f + 1) * P]).then_inc(wb_in[f % 2], 16)
                    if f == 1:
                        sp.dma_start(gain[:], io["ln1_g"].to_broadcast([P, D])).then_inc(ln_in, 16)
                        sp.dma_start(offset[:], io["ln1_b"].to_broadcast([P, D])).then_inc(ln_in, 16)
                        sp.dma_start(wo[:], io["w_out"].rearrange("(k p) n -> p k n", p=P)).then_inc(wo_in, 16)
                for t in range(TILES):
                    R = ROWS[t]
                    if t >= 2:
                        sp.wait_ge(mix_used, t - 1)
                    src = io["x_p"][t * P:(t + 1) * P, :] if t < SAMPLE else io["x_s"]
                    sp.dma_start(xt[0:R, t % 2, :], src).then_inc(xt_in[t % 2], 16)

            @block.tensor
            def _(pe):
                for f in range(KD):
                    pe.wait_ge(wb_in[f % 2], 64 * (f // 2 + 1))
                    for c, (a, b) in enumerate(TC):
                        n = f * 3 + c
                        bank = 4 * (n % 2)
                        if n >= 2:
                            pe.wait_ge(m_ready, n - 1)
                        for g, lo, kn, rhs in ((0, 0, 8, xT), (1, 8, 8, xT), (2, 16, 4, res["oaT"]), (3, 20, 4, res["obT"])):
                            for kk in range(kn):
                                last = pe.matmul(pm[:, bank + g, 0:b - a], wb[:, f % 2, lo + kk, :], rhs[:, kk, a:b],
                                                 start=(kk == 0), stop=(kk == kn - 1))
                        last.then_inc(g_ready, 1)
                pe.wait_ge(m_ready, 3 * KD)
                pe.wait_ge(wo_in, 16)

                def transposes(t):
                    R = ROWS[t]
                    pe.wait_ge(h_ready, t + 1)
                    if t >= 1:
                        pe.wait_ge(ht_copied, t)
                    for kk in range(KD):
                        last = pe.transpose(pm[:, 4 + kk // 4, (kk % 4) * P:(kk % 4) * P + R], res["h1"][0:R, t, kk * P:(kk + 1) * P], ident[0:R, 0:R])
                    last.then_inc(ht_ready, 1)

                for t in range(TILES):
                    R = ROWS[t]
                    if t >= 2:
                        pe.wait_ge(mix_used, t - 1)
                    for c in range(2):
                        for kk in range(KD):
                            last = pe.matmul(pm[0:R, 2 * (t % 2) + c, :], mT[:, kk, tok(t)], wo[:, kk, c * 512:(c + 1) * 512],
                                             start=(kk == 0), stop=(kk == KD - 1))
                    last.then_inc(mix_ready, 1)
                    if t >= 1:
                        transposes(t - 1)
                transposes(SAMPLE)

            @block.scalar
            def _(act):
                for n in range(3 * KD):
                    act.wait_ge(g_ready, n + 1)
                    if n >= 2:
                        act.wait_ge(m_ready, n - 1)
                    act.activation(sg[:, n % 2, :, :], pm[:, 4 * (n % 2):4 * (n % 2) + 2, 0:352], ACT.Sigmoid).then_inc(sig_done, 1)

                def copies(t):
                    R = ROWS[t]
                    act.wait_ge(ht_ready, t + 1)
                    act.copy(res["h1T"][:, :, tok(t)], pm[:, 4:6, :].rearrange("p a (b r) -> p (a b) r", r=P)[:, :, 0:R]).then_inc(ht_copied, 1)

                for t in range(TILES):
                    R = ROWS[t]
                    act.wait_ge(root_asked, t + 1)
                    act.activation(mv[0:R, 1:2], mv[0:R, 1:2], ACT.Sqrt).then_inc(root_given, 1)
                    if t >= 1:
                        copies(t - 1)
                copies(SAMPLE)

            @block.vector
            def _(dve):
                link = Link(dve, g_step)
                for n in range(3 * KD):
                    f, (a, b) = n // 3, TC[n % 3]
                    bank = 4 * (n % 2)
                    dve.wait_ge(sig_done, n + 1)
                    if n >= 1:
                        dve.wait_ge(m_ready, n)
                    link.add(dve.tensor_tensor(pr[:, :, :], sg[:, n % 2, :, :], pm[:, bank + 2:bank + 4, 0:352], ALU.mult))
                    link.wait()
                    dve.tensor_tensor(mT[:, f, a:b], pr[:, 0, :], pr[:, 1, :], ALU.add).then_inc(m_ready, 1)
                dve.wait_ge(ln_in, 32)
                for t in range(TILES):
                    R = ROWS[t]
                    x = res["h1"][0:R, t, :]
                    dve.wait_ge(mix_ready, t + 1)
                    dve.wait_ge(xt_in[t % 2], 16 * (t // 2 + 1))
                    dve.scalar_tensor_tensor(x, xt[0:R, t % 2, :], ALPHA, pm[0:R, 2 * (t % 2):2 * (t % 2) + 2, :].rearrange("p a b -> p (a b)"),
                                             ALU.mult, ALU.add).then_inc(mix_used, 1)
                    dve.wait_ge(mix_used, t + 1)
                    if t >= 1:
                        dve.wait_ge(h_ready, t)
                    layer_norm(dve, link, x, st, mv, gain, offset, R, root_asked, root_given, t).then_inc(h_ready, 1)


def choose_experts(nc, io, res, sem):
    with ExitStack() as ctx:
        def sb(name, shape, dt=F32):
            return ctx.enter_context(nc.sbuf_tensor(name, shape, dt))
        wq = sb("w_pq_sb", [P, 2, KD, P])
        pk = sb("pk_sb", [P, 2 * PH, P])
        qT = sb("pqT", [P, 2, NT])
        sc = sb("key_scores", [P, TILES, 2 * PH, P])
        v = sb("key_top", [P, 2 * PH, PK])
        iu = sb("key_at", [P, 2 * PH, PK], U32)
        fi = sb("key_at_f", [P, 2 * PH, PK])
        cand = sb("cand", [P, PH, NCAND])
        cidx = sb("cand_e", [P, PH, NCAND])
        top = sb("top", [P, PH, PK])
        tat = sb("top_at", [P, PH, PK], U32)
        taf = sb("top_at_f", [P, PH, PK])
        ef = sb("expert_f", [P, PH, PK])
        hot = sb("one_hot", [P, 4, PK, NCAND])
        iota = sb("iota_sb", [P, NCAND])
        tot = sb("total", [P, PH])
        pq = ctx.enter_context(nc.psum_tensor("pq_ps", [P, 3, 512], F32))
        pss = ctx.enter_context(nc.psum_tensor("key_ps", [P, 3, 512], F32))
        (pk_in, wq_used, q_ready, q_copied, s_ready, s_copied, step, e_asked, e_given) = (sem(n) for n in (
            "pk_in", "w_pq_used", "pq_ready", "pq_copied", "key_ready", "key_copied", "pick_step", "exp_asked", "exp_given"))
        wq_in = [sem("w_pq_in0"), sem("w_pq_in1")]
        TC = [(0, 352), (352, 704), (704, 1056)]
        NB = 2 * PH

        with nc.Block() as block:
            @block.sync
            def _(sp):
                sp.dma_start(pk[:], io["pkT"]).then_inc(pk_in, 16)
                sp.dma_start(iota[:], io["iota"]).then_inc(pk_in, 16)
                wv = io["w_pq"].rearrange("(k p) n -> p k n", p=P)
                for b in range(NB):
                    if b >= 2:
                        sp.wait_ge(q_ready, b - 1)
                    sp.dma_start(wq[:, b % 2, :, :], wv[:, :, b * P:(b + 1) * P]).then_inc(wq_in[b % 2], 16)

            @block.tensor
            def _(pe):
                pe.wait_ge(pk_in, 32)

                def key_scores(b):
                    pe.wait_ge(q_copied, b + 1)
                    if b >= 1:
                        pe.wait_ge(s_copied, b)
                    for t in range(TILES):
                        last = pe.matmul(pss[0:ROWS[t], t // 4, (t % 4) * P:(t % 4 + 1) * P], qT[:, b % 2, tok(t)], pk[:, b, :], start=True, stop=True)
                    last.then_inc(s_ready, 1)

                for b in range(NB):
                    pe.wait_ge(wq_in[b % 2], 16 * (b // 2 + 1))
                    if b >= 1:
                        pe.wait_ge(q_copied, b)
                    for c, (a, e) in enumerate(TC):
                        for kk in range(KD):
                            last = pe.matmul(pq[:, c, 0:e - a], wq[:, b % 2, kk, :], res["h1T"][:, kk, a:e], start=(kk == 0), stop=(kk == KD - 1))
                    last.then_inc(q_ready, 1)
                    key_scores(b)

            @block.scalar
            def _(act):
                for b in range(NB):
                    act.wait_ge(q_ready, b + 1)
                    if b >= 2:
                        act.wait_ge(s_ready, b - 1)
                    act.copy(qT[:, b % 2, :].rearrange("p (c n) -> p c n", c=3), pq[:, :, 0:352]).then_inc(q_copied, 1)
                    act.wait_ge(s_ready, b + 1)
                    act.copy(sc[:, 0:8, b, :], pss[:, 0:2, :].rearrange("p a (t n) -> p (a t) n", n=P))
                    act.copy(sc[0:TS, SAMPLE, b, :], pss[0:TS, 2, 0:P]).then_inc(s_copied, 1)
                for t in range(TILES):
                    R = ROWS[t]
                    act.wait_ge(e_asked, t + 1)
                    act.activation(top[0:R], top[0:R], ACT.Exp).then_inc(e_given, 1)

            @block.vector
            def _(dve):
                link = Link(dve, step)
                dve.wait_ge(pk_in, 32)
                dve.wait_ge(s_copied, NB)

                def top16(values, at, work, n):
                    for x in range(n):
                        link.add(dve.max(values(x)[:, 0:8], work(x)))
                    link.wait()
                    for x in range(n):
                        link.add(dve.max_index(at(x)[:, 0:8], values(x)[:, 0:8], work(x)))
                    link.wait()
                    for x in range(n):
                        link.add(dve.match_replace(work(x), values(x)[:, 0:8], work(x), GONE))
                    link.wait()
                    for x in range(n):
                        link.add(dve.max(values(x)[:, 8:16], work(x)))
                    link.wait()
                    for x in range(n):
                        link.add(dve.max_index(at(x)[:, 8:16], values(x)[:, 8:16], work(x)))
                    link.wait()

                for t in range(TILES):
                    R = ROWS[t]
                    link.wait()
                    top16(lambda x: v[0:R, x, :], lambda x: iu[0:R, x, :], lambda x: sc[0:R, t, x, :], NB)
                    link.add(dve.tensor_copy(fi[0:R], iu[0:R]))
                    link.wait()
                    i1 = fi[0:R].rearrange("p (h two) k -> p h two k", two=2)
                    vv = v[0:R].rearrange("p (h two) k -> p h two k", two=2)
                    link.add(dve.tensor_scalar(i1[:, :, 0, :], i1[:, :, 0, :], float(NKEYS), None, ALU.mult))
                    link.wait()
                    for src, dst in ((vv, cand), (i1, cidx)):
                        for i, m, n, o in stair_runs():
                            for x in range(m) if n > 1 else (0,):
                                if n > 1:
                                    out = dst[0:R, :, o + x * n:o + (x + 1) * n]
                                    a = src[:, :, 0, i + x:i + x + 1].to_broadcast([R, PH, n])
                                    b = src[:, :, 1, 0:n]
                                else:
                                    out = dst[0:R, :, o:o + m]
                                    a = src[:, :, 0, i:i + m]
                                    b = src[:, :, 1, 0:1].to_broadcast([R, PH, m])
                                link.add(dve.tensor_tensor(out, a, b, ALU.add))
                    link.wait()
                    top16(lambda x: top[0:R, x, :], lambda x: tat[0:R, x, :], lambda x: cand[0:R, x, :], PH)
                    link.add(dve.tensor_copy(taf[0:R], tat[0:R]))
                    link.wait()
                    for x in range(0, PH, 4):
                        for y in range(4):
                            link.add(dve.tensor_tensor(hot[0:R, y], iota[0:R, :].unsqueeze(1).to_broadcast([R, PK, NCAND]),
                                                       taf[0:R, x + y, :].unsqueeze(2).to_broadcast([R, PK, NCAND]), ALU.is_equal))
                        link.wait()
                        for y in range(4):
                            link.add(dve.tensor_tensor(hot[0:R, y], hot[0:R, y], cidx[0:R, x + y, :].unsqueeze(1).to_broadcast([R, PK, NCAND]), ALU.mult))
                        link.wait()
                        link.add(dve.tensor_reduce(ef[0:R, x:x + 4, :], hot[0:R], AX.X, ALU.add))
                        link.wait()
                    link.add(dve.tensor_copy(res["expert"][0:R, t, :].rearrange("p (h k) -> p h k", k=PK), ef[0:R]))
                    link.add(dve.tensor_copy(tot[0:R, :].unsqueeze(2), top[0:R, :, 0:1]))
                    link.wait()
                    dve.tensor_tensor(top[0:R], top[0:R], tot[0:R, :].unsqueeze(2).to_broadcast([R, PH, PK]), ALU.subtract).then_inc(e_asked, 1)
                    dve.wait_ge(e_given, t + 1)
                    link.add(dve.tensor_reduce(tot[0:R, :], top[0:R], AX.X, ALU.add))
                    link.wait()
                    link.add(dve.reciprocal(tot[0:R, :], tot[0:R, :]))
                    link.wait()
                    link.add(dve.tensor_tensor(res["weight"][0:R, t, :].rearrange("p (h k) -> p h k", k=PK), top[0:R],
                                               tot[0:R, :].unsqueeze(2).to_broadcast([R, PH, PK]), ALU.mult))


def run_experts(nc, io, res, sem):
    with ExitStack() as ctx:
        def sb(name, shape, dt=F32):
            return ctx.enter_context(nc.sbuf_tensor(name, shape, dt))
        U = sb("u_rows", [P, PK, D])
        V = sb("v_rows", [P, PK - 4, D])
        spare = res["xT"][:].rearrange("p k n -> p (k n)")[:, 0:8 * D].rearrange("p (x d) -> p x d", d=D)

        def urow(j):
            return U[:, j, :]

        def vrow(j):
            return V[:, j, :] if j < PK - 4 else spare[:, j - (PK - 4), :]
        at = sb("rows_at", [P, 2, PK], U32)
        dots = sb("dots", [P, PK])
        gl = sb("gelu", [P, PK])
        wt = sb("expert_w", [P, PK])
        dg = sb("diag", [P, 4, P])
        zero = sb("zero", [P, P])
        ai = sb("alpha_ident", [P, P])
        y, gain, offset, hT = (spare[:, 4 + x, :] for x in range(4))
        st, mv = sb("ln2_st", [P, 12]), sb("ln2_mv", [P, 2])
        acc = ctx.enter_context(nc.psum_tensor("acc", [P, D], F32))
        ident = res["ident"]
        u_in = [sem(f"u_in{j}") for j in range(PK)]
        v_in = [sem(f"v_in{j}") for j in range(PK)]
        (ln_in, at_set, slot_seen, dve_seen, pe_seen, h_set, dot_done, gelu_done, w_done, diag_done, v_used, sum_open, sum_done, y_step, y_ready, y_out,
         root_asked, root_given, const_set) = (sem(n) for n in (
            "ln2_in", "at_set", "slot_seen", "dve_seen", "pe_seen", "h_set", "dot_done", "gelu_done", "w_done", "diag_done", "v_used", "sum_open", "sum_done",
            "y_step", "y_ready", "y_out", "root2_asked", "root2_given", "const_set"))
        MAIN = TILES - 1

        with nc.Block() as block:
            @block.sync
            def _(sp):
                sp.dma_start(gain, io["ln2_g"].to_broadcast([P, D])).then_inc(ln_in, 16)
                sp.dma_start(offset, io["ln2_b"].to_broadcast([P, D])).then_inc(ln_in, 16)
                with sp.Fori(0, MAIN) as t:
                    sp.wait_ge(y_ready, t + 1)
                    sp.dma_start(io["y_p"][bass.ds(t * P, P), :], y).then_inc(y_out, 16)
                sp.wait_ge(y_ready, TILES)
                sp.dma_start(io["y_s"], y[0:TS, :]).then_inc(y_out, 16)
                sp.wait_ge(y_out, 16 * TILES)

            @block.gpsimd
            def _(pool):
                experts = res["expert"][:].rearrange("p t k -> p (t k)")

                def gathers(n, b, R, rows, table, landed, used, first):
                    for j in range(PK):
                        if not first:
                            pool.wait_ge(used, n * PK + (j + 1 - PK))
                            pool.sem_inc(slot_seen, 1)
                        pool.indirect_dma_start(out=rows(j)[0:R, :], out_offset=None, in_=table,
                                                in_offset=bass.IndirectOffsetOnAxis(ap=at[0:R, b, j:j + 1], axis=0)).then_inc(landed[j], 16)

                def head(n, b, R, first=False):
                    pool.tensor_copy(at[0:R, b, :], experts[0:R, bass.ds(n * PK, PK)]).then_inc(at_set, 1)
                    pool.wait_ge(at_set, n + 1)
                    pool.sem_inc(slot_seen, 1)
                    gathers(n, b, R, urow, io["pu"], u_in, dot_done, first)
                    gathers(n, b, R, vrow, io["pv"], v_in, v_used, first)

                head(0, 0, P, first=True)
                head(1, 1, P)
                for start, stop, R in ((1, MAIN * PH // 2, P), (MAIN * PH // 2, TILES * PH // 2, TS)):
                    with pool.Fori(start, stop) as pair:
                        for b in range(2):
                            pool.wait_ge(v_in[PK - 1], pair * 32 + (16 * b - 16))
                            head(pair * 2 + b, b, R)

            @block.vector
            def _(dve):
                link = Link(dve, const_set)
                link.add(dve.memset(zero[:], 0.0))
                link.add(dve.tensor_scalar(ai[:], ident[:], ALPHA, None, ALU.mult))
                link.wait()
                dve.wait_ge(ln_in, 32)
                OPS = 7

                def heads(n, R, t, h):
                    for j in range(PK):
                        dve.wait_ge(u_in[j], n * 16 + 16)
                        dve.tensor_tensor_reduce(U[0:R, j, :], U[0:R, j, :], hT[0:R, :], 1.0, 0.0, ALU.mult, ALU.add,
                                                 dots[0:R, j:j + 1]).then_inc(dot_done, 1)
                    dve.wait_ge(gelu_done, n + 1)
                    w = res["weight"][:].rearrange("p t k -> p (t k)")[0:R, bass.ds(n * PK, PK)]
                    dve.tensor_tensor(wt[0:R, :], gl[0:R, :], w, ALU.mult).then_inc(w_done, 1)

                def tile(t, R, first):
                    src = res["h1"][:].rearrange("p t d -> p (t d)")[0:R, bass.ds(t * D, D)]
                    if not first:
                        dve.wait_ge(y_ready, t + 0)
                    dve.tensor_copy(hT[0:R, :], src).then_inc(h_set, 1)
                    dve.wait_ge(h_set, t + 1)
                    dve.sem_inc(dve_seen, 1)

                def finish(t, R, first):
                    dve.wait_ge(sum_done, t + 1)
                    if not first:
                        dve.wait_ge(y_out, t * 16)
                    base = [0]

                    def add(ins):
                        base[0] += 1
                        ins.then_inc(y_step, 1)
                        dve.wait_ge(y_step, t * OPS + base[0])
                    yv = y[0:R, :]
                    add(dve.tensor_copy(yv, acc[0:R, :]))
                    add(dve.bn_stats(st[0:R, 0:6], yv[:, 0:512]))
                    add(dve.bn_stats(st[0:R, 6:12], yv[:, 512:1024]))
                    dve.sem_inc(dve_seen, 1)
                    add(dve.bn_aggr(mv[0:R, 0:2], st[0:R, :]))
                    dve.tensor_scalar(mv[0:R, 1:2], mv[0:R, 1:2], EPS, None, ALU.add).then_inc(root_asked, 1)
                    dve.wait_ge(root_given, t + 1)
                    add(dve.reciprocal(mv[0:R, 1:2], mv[0:R, 1:2]))
                    add(dve.tensor_scalar(yv, yv, mv[0:R, 0:1], mv[0:R, 1:2], ALU.subtract, ALU.mult))
                    add(dve.tensor_tensor(yv, yv, gain[0:R, :], ALU.mult))
                    dve.tensor_tensor(yv, yv, offset[0:R, :], ALU.add).then_inc(y_ready, 1)
                    assert base[0] == OPS

                tile(0, P, True)
                with dve.Fori(0, PH) as h:
                    heads(h, P, 0, h)
                finish(0, P, True)
                with dve.Fori(1, MAIN) as t:
                    tile(t, P, False)
                    with dve.Fori(0, PH) as h:
                        heads(t * PH + h, P, t, h)
                    finish(t, P, False)
                tile(SAMPLE, TS, False)
                with dve.Fori(0, PH) as h:
                    heads(SAMPLE * PH + h, TS, SAMPLE, h)
                finish(SAMPLE, TS, False)

            @block.scalar
            def _(act):
                def heads(n, R, first):
                    act.wait_ge(dot_done, n * PK + PK)
                    if not first:
                        act.wait_ge(w_done, n + 0)
                        act.wait_ge(diag_done, n * PK)
                    act.activation(gl[0:R, :], dots[0:R, :], ACT.Gelu).then_inc(gelu_done, 1)
                    act.wait_ge(w_done, n + 1)
                    for j in range(PK):
                        if j >= 4 or not first:
                            act.wait_ge(v_used, n * PK + (j - 3))
                        act.activation(dg[0:R, j % 4, 0:R], ident[0:R, 0:R], ACT.Copy, scale=wt[0:R, j:j + 1]).then_inc(diag_done, 1)

                def root(t, R):
                    act.wait_ge(root_asked, t + 1)
                    act.activation(mv[0:R, 1:2], mv[0:R, 1:2], ACT.Sqrt).then_inc(root_given, 1)
                heads(0, P, True)
                with act.Fori(1, PH) as h:
                    heads(h, P, False)
                root(0, P)
                with act.Fori(1, MAIN) as t:
                    with act.Fori(0, PH) as h:
                        heads(t * PH + h, P, False)
                    root(t, P)
                with act.Fori(0, PH) as h:
                    heads(SAMPLE * PH + h, TS, False)
                root(SAMPLE, TS)

            @block.tensor
            def _(pe):
                pe.wait_ge(const_set, 2)

                def tile(t, R, first):
                    pe.wait_ge(h_set, t + 1)
                    for c in range(2):
                        pe.matmul(acc[0:R, c * 512:(c + 1) * 512], ai[0:R, 0:R], hT[0:R, c * 512:(c + 1) * 512], start=True, stop=False)

                def heads(n, R):
                    for j in range(PK):
                        pe.wait_ge(diag_done, n * PK + j + 1)
                        pe.wait_ge(v_in[j], n * 16 + 16)
                        if R < P:
                            pe.sem_inc(pe_seen, 1)
                        for c in range(2):
                            last = pe.matmul(acc[0:R, c * 512:(c + 1) * 512], dg[0:R, j % 4, 0:R], vrow(j)[0:R, c * 512:(c + 1) * 512],
                                             start=False, stop=False)
                        last.then_inc(v_used, 1)

                def close(R):
                    for c in range(2):
                        last = pe.matmul(acc[0:R, c * 512:(c + 1) * 512], zero[0:R, 0:R], hT[0:R, c * 512:(c + 1) * 512], start=False, stop=True)
                    last.then_inc(sum_done, 1)
                with pe.Fori(0, MAIN) as t:
                    tile(t, P, False)
                    with pe.Fori(0, PH) as h:
                        heads(t * PH + h, P)
                    close(P)
                tile(SAMPLE, TS, False)
                with pe.Fori(0, PH) as h:
                    heads(SAMPLE * PH + h, TS)
                close(TS)


def streaming_step(nc, io):
    with ExitStack() as ctx:
        def sb(name, shape, dt=F32):
            return ctx.enter_context(nc.sbuf_tensor(name, shape, dt))

        def sem(name):
            return ctx.enter_context(nc.semaphore(name))
        res = {"ident": sb("ident_sb", [P, P]), "xT": sb("xT_sb", [P, KD, NT]), "late": sb("late", [P, TILES * D]),
               "expert": sb("expert", [P, TILES, PH * PK], U32), "weight": sb("weight", [P, TILES, PH * PK])}
        res["oaT"] = res["late"][:, 0:4 * NT].rearrange("p (k n) -> p k n", k=4)
        res["obT"] = res["late"][:, 4 * NT:8 * NT].rearrange("p (k n) -> p k n", k=4)
        res["h1"] = res["late"][:].rearrange("p (t d) -> p t d", t=TILES)
        res["h1T"] = res["xT"]
        load_common(nc, io, res, sem)
        gated_linear(nc, io, res, sem)
        with ExitStack() as att:
            def own(name, shape):
                return att.enter_context(nc.sbuf_tensor(name, shape, F32))
            res |= {"aqT": own("aqT", [P, GROUP, NT]), "iqT": own("iqT", [P, 2, NT]), "iw": own("iw", [P, TILES, IH]),
                    "kT": own("kT", [P, TP]), "ikT": own("ikT", [P, TP]), "V": own("V", [P, TP // P, P]),
                    "kTs": own("kTs", [P, PAST + TS]), "ikTs": own("ikTs", [P, PAST + TS]), "Vs": own("Vs", [P, PAST // P + 1, P])}
            project_attention(nc, io, res, sem)
            sparse_attention(nc, io, res, sem)
        merge(nc, io, res, sem)
        choose_experts(nc, io, res, sem)
        run_experts(nc, io, res, sem)


def load_common(nc, io, res, sem):
    common_in = sem("common_in")
    with nc.Block() as block:
        @block.sync
        def _(sp):
            sp.dma_start(res["ident"][:], io["ident"]).then_inc(common_in, 16)
            sp.dma_start(res["xT"][:], io["xT"]).then_inc(common_in, 16)
            sp.wait_ge(common_in, 32)


def constants(np):
    half = HD // 2
    inv = np.float32(10000.0) ** (-np.arange(half, dtype=np.float32) / np.float32(half))
    pos = np.concatenate([np.arange(TP), PAST + np.arange(TS)]).astype(np.float32)
    ang = (pos[:, None] * inv[None, :]).astype(np.float32)

    def tiles(a):
        out = np.zeros((P, TILES, a.shape[1]), np.float32)
        for t in range(TILES):
            out[:ROWS[t], t] = a[t * P:t * P + ROWS[t]]
        return out
    cos, sin = np.cos(ang), np.sin(ang)
    s, t = np.arange(P)[:, None], np.arange(P)[None, :]
    reset = np.ones((P, NT), np.float32)
    reset[:, ::GC] = 0.0
    return {
        "ident": np.eye(P, dtype=np.float32),
        "cos": tiles(np.concatenate([cos, cos], 1)), "sin": tiles(np.concatenate([-sin, sin], 1)),
        "gla_mask": ((s <= t) & (s // GC == t // GC)).astype(np.float32), "reset": reset,
        "iota": np.tile(np.arange(NCAND, dtype=np.float32), (P, 1)),
    }


OUTS = {"y_p": (TP, D), "y_s": (TS, D), "k_p": (TP, KV * HD), "v_p": (TP, KV * HD), "ik_p": (TP, ID),
        "gla_p": (GH, GK, GK), "k_s": (TS, KV * HD), "v_s": (TS, KV * HD), "ik_s": (TS, ID), "gla_s": (GH, GK, GK)}


def layouts(np, v):
    x = np.concatenate([v["x_prompt"][0], v["x_sample"][0]], 0)
    keys = np.stack([v["pk1"][0], v["pk2"][0]], 1).reshape(2 * PH, NKEYS, P)
    ik = v["cache_idx_k"][0, 0].T
    return {
        "xT": x.T.reshape(KD, P, NT).transpose(1, 0, 2), "x_p": v["x_prompt"][0], "x_s": v["x_sample"][0],
        "kcT": v["cache_k"][0, 0].reshape(PAST, KV * HD).T, "ikcT": np.concatenate([ik, ik], 0),
        "vc": v["cache_v"][0, 0].reshape(PAST, KV * HD), "state": v["state_gla"][0, 0],
        "w_in": v["w_in"][0], "w_fa": v["w_fa"][0], "b_fa": v["b_fa"][0].reshape(GH, GK).T, "g_gla_norm": v["g_gla_norm"],
        "w_pa": v["w_pa"][0], "w_pb": v["w_pb"][0], "w_out": v["w_out"][0], "w_pq": v["w_pq"][0],
        "pkT": keys.transpose(2, 0, 1), "pu": v["pu"][0], "pv": v["pv"][0],
        "ln1_g": v["ln1_g"], "ln1_b": v["ln1_b"], "ln2_g": v["ln2_g"], "ln2_b": v["ln2_b"],
    }


def kernel(**inputs):
    import numpy as np
    import concourse.bacc as bacc
    from concourse.bass_utils import run_bass_kernel_spmd

    arrays = {n: np.ascontiguousarray(a) for n, a in (layouts(np, inputs) | constants(np)).items()}
    nc = bacc.Bacc("TRN2", target_bir_lowering=False, num_devices=1)
    io = {n: nc.dram_tensor(f"in_{n}", a.shape, F32, kind="ExternalInput").ap() for n, a in arrays.items()}
    io |= {n: nc.dram_tensor(f"out_{n}", s, F32, kind="ExternalOutput").ap() for n, s in OUTS.items()}
    streaming_step(nc, io)
    r = run_bass_kernel_spmd(nc, [{f"in_{n}": a for n, a in arrays.items()}], core_ids=[0]).results[0]
    o = {n: r[f"out_{n}"] for n in OUTS}
    return (o["y_p"].reshape(1, TP, D), o["y_s"].reshape(1, TS, D),
            o["k_p"].reshape(1, 1, TP, KV, HD), o["v_p"].reshape(1, 1, TP, KV, HD), o["ik_p"].reshape(1, 1, TP, ID),
            o["gla_p"].reshape(1, 1, GH, GK, GK),
            o["k_s"].reshape(1, 1, TS, KV, HD), o["v_s"].reshape(1, 1, TS, KV, HD), o["ik_s"].reshape(1, 1, TS, ID),
            o["gla_s"].reshape(1, 1, GH, GK, GK))
```

```python
from contextlib import ExitStack

import concourse.bass as bass
from concourse import mybir

F32 = mybir.dt.float32
U32 = mybir.dt.uint32
ALU = mybir.AluOpType
ACT = mybir.ActivationFunctionType
AX = mybir.AxisListType

P = 128
D = 1024
KD = D // P
TP = 1024
TS = 32
PAST = 512
NT = TP + TS
TILES = TP // P + 1
SAMPLE = TILES - 1
ROWS = [P] * (TILES - 1) + [TS]
CHUNK = 64
HEADS, KV, HD, GROUP = 8, 2, 64, 4
IH, ID = 4, 64
TOPK_P = min(256, TP // 4)
TOPK_S = min(256, (PAST + TS) // 4)
GH, GK = 4, 128
GC = 32
NCH = NT // GC
TAU = 16.0
LOWRANK = 16
PH, NKEYS, PK = 8, 128, 16
NEXP = NKEYS * NKEYS
EPS = 1e-5
ALPHA = 2.0 ** 0.25
C_AV, C_IQ, C_IW, C_GQ, C_GK, C_GV, C_GF, C_GR, C_GATE = 640, 768, 1088, 1092, 1604, 2116, 2628, 2644, 3156
DSA = C_GQ
GONE = -3.0e38
STAIR = [PK // (i + 1) for i in range(PK)]
STAIR_AT = [sum(STAIR[:i]) for i in range(PK)]
NCAND = sum(STAIR)


def stair_runs():
    runs, i = [], 0
    while i < PK:
        n = sum(1 for k in STAIR[i:] if k == STAIR[i])
        runs.append((i, n, STAIR[i], STAIR_AT[i]))
        i += n
    return runs


def tok(t):
    return slice(t * P, t * P + ROWS[t])


class Link:

    def __init__(self, eng, sem):
        self.eng, self.sem, self.n = eng, sem, 0

    def add(self, ins):
        self.n += 1
        ins.then_inc(self.sem, 1)

    def wait(self):
        if self.n:
            self.eng.wait_ge(self.sem, self.n)


def project_attention(nc, io, res, sem):
    with ExitStack() as ctx:
        def sb(name, shape):
            return ctx.enter_context(nc.sbuf_tensor(name, shape, F32))
        w = sb("w_dsa", [P, KD, DSA])
        z = sb("z", [P, 2, DSA])
        ta = sb("rope_a", [P, 960])
        tb = sb("rope_b", [P, 960])
        rot = sb("rot", [P, 2, 1024])
        cos = res["tail"][:, 0:TILES * HD].rearrange("p (t d) -> p t d", d=HD)
        sin = sb("sin_sb", [P, TILES, HD])
        zps = ctx.enter_context(nc.psum_tensor("zps", [P, 2, 3 * 512], F32))
        tps = ctx.enter_context(nc.psum_tensor("tps", [P, 1024], F32))
        ident, xT = res["ident"], res["xT"]
        consts_in, w_in_, sample_in = sem("consts_in"), [sem(f"w_dsa_in{c}") for c in range(3)], sem("sample_in")
        z_ready, z_copied, rope_step, rot_ready = sem("z_ready"), sem("z_copied"), sem("rope_step"), sem("rot_ready")
        turned, turned_copied, kv_out = sem("turned"), sem("turned_copied"), [sem("kv_out0"), sem("kv_out1")]
        bounds = [(0, 512), (512, 1024), (1024, DSA)]

        with nc.Block() as block:
            @block.sync
            def _(sp):
                wv = io["w_in"].rearrange("(k p) n -> p k n", p=P)
                for c, (a, b) in enumerate(bounds):
                    sp.dma_start(w[:, :, a:b], wv[:, :, a:b]).then_inc(w_in_[c], 16)
                for dst, src in ((cos, io["cos"]), (sin[:], io["sin"])):
                    sp.dma_start(dst, src).then_inc(consts_in, 16)
                sp.dma_start(res["kTs"][:, 0:PAST], io["kcT"]).then_inc(sample_in, 16)
                sp.dma_start(res["ikTs"][:, 0:PAST], io["ikcT"]).then_inc(sample_in, 16)
                sp.dma_start(res["Vs"][:, 0:PAST // P, :], io["vc"].rearrange("(c p) n -> p c n", p=P)).then_inc(sample_in, 16)
                for t in range(TILES):
                    R = ROWS[t]
                    k_o, v_o, ik_o = (io["k_p"], io["v_p"], io["ik_p"]) if t < SAMPLE else (io["k_s"], io["v_s"], io["ik_s"])
                    row = slice(t * P, t * P + R) if t < SAMPLE else slice(0, R)
                    sp.wait_ge(rot_ready, t + 1)
                    sp.wait_ge(z_copied, t + 1)
                    v_src = res["V"][:, t, :] if t < SAMPLE else res["Vs"][0:R, PAST // P, :]
                    sp.dma_start(k_o[row, :], rot[0:R, t % 2, 512:640]).then_inc(kv_out[t % 2], 16)
                    sp.dma_start(ik_o[row, :], rot[0:R, t % 2, 896:960]).then_inc(kv_out[t % 2], 16)
                    sp.dma_start(v_o[row, :], v_src).then_inc(kv_out[t % 2], 16)
                for b in range(2):
                    sp.wait_ge(kv_out[b], 48 * len(range(b, TILES, 2)))
                sp.wait_ge(sample_in, 48)

            @block.tensor
            def _(pe):
                def transposes(t):
                    R = ROWS[t]
                    pe.wait_ge(rot_ready, t + 1)
                    if t:
                        pe.wait_ge(turned_copied, t)
                    for b in range(8):
                        last = pe.transpose(tps[:, b * P:b * P + R], rot[0:R, t % 2, b * P:(b + 1) * P], ident[0:R, 0:R])
                    last.then_inc(turned, 1)

                for t in range(TILES):
                    if t >= 2:
                        pe.wait_ge(z_copied, t - 1)
                    for c, (a, b) in enumerate(bounds):
                        if t == 0:
                            pe.wait_ge(w_in_[c], 16)
                        for k in range(KD):
                            last = pe.matmul(zps[0:ROWS[t], t % 2, c * 512:c * 512 + b - a], xT[:, k, tok(t)], w[:, k, a:b],
                                             start=(k == 0), stop=(k == KD - 1))
                    last.then_inc(z_ready, 1)
                    if t >= 1:
                        transposes(t - 1)
                transposes(SAMPLE)

            @block.scalar
            def _(act):
                def copies(t):
                    R = ROWS[t]
                    act.wait_ge(turned, t + 1)
                    tv = tps[:].rearrange("p (b r) -> p b r", b=8)[:, :, 0:R]
                    s = tok(t)
                    act.copy(res["aqT"][:, :, s], tv[:, 0:4, :])
                    act.copy(res["iqT"][:, :, s], tv[:, 5:7, :])
                    kT, ikT, at = (res["kT"], res["ikT"], t * P) if t < SAMPLE else (res["kTs"], res["ikTs"], PAST)
                    act.copy(kT[:, at:at + R], tv[:, 4, :])
                    act.copy(ikT[:, at:at + R], tv[:, 7, :]).then_inc(turned_copied, 1)

                for t in range(TILES):
                    R = ROWS[t]
                    act.wait_ge(z_ready, t + 1)
                    if t >= 2:
                        act.wait_ge(rot_ready, t - 1)
                    act.copy(z[0:R, t % 2, :], zps[0:R, t % 2, 0:DSA])
                    v_dst = res["V"][:, t, :] if t < SAMPLE else res["Vs"][0:R, PAST // P, :]
                    act.copy(v_dst, zps[0:R, t % 2, C_AV:C_IQ])
                    act.mul(res["iw"][0:R, t, :], zps[0:R, t % 2, C_IW:DSA], IH ** -0.5 * ID ** -0.5).then_inc(z_copied, 1)
                    if t >= 1:
                        copies(t - 1)
                copies(SAMPLE)

            @block.vector
            def _(dve):
                link = Link(dve, rope_step)
                dve.wait_ge(consts_in, 32)
                for t in range(TILES):
                    R, b = ROWS[t], t % 2
                    dve.wait_ge(z_copied, t + 1)
                    if t >= 1:
                        dve.wait_ge(rot_ready, t)
                    for z0, n, o in ((0, 10, 0), (C_IQ, 5, 640)):
                        zv = z[0:R, b, z0:z0 + n * HD].rearrange("p (h d) -> p h d", d=HD)
                        av = ta[0:R, o:o + n * HD].rearrange("p (h d) -> p h d", d=HD)
                        bv = tb[0:R, o:o + n * HD].rearrange("p (h d) -> p h d", d=HD)
                        cv = cos[0:R, t:t + 1, :].to_broadcast([R, n, HD])
                        dve.tensor_tensor(av, zv, cv, ALU.mult)
                        for lo, hi in ((0, 32), (32, 0)):
                            sv = sin[0:R, t:t + 1, lo:lo + 32].to_broadcast([R, n, 32])
                            last = dve.tensor_tensor(bv[:, :, lo:lo + 32], zv[:, :, hi:hi + 32], sv, ALU.mult)
                    link.add(last)
                    link.wait()
                    if t >= 2:
                        dve.wait_ge(turned, t - 1)
                        dve.wait_ge(kv_out[b], 48 * (t // 2))
                    dve.tensor_tensor(rot[0:R, b, 0:512].rearrange("p (g n d) -> p n g d", g=GROUP, n=KV),
                                      ta[0:R, 0:512].rearrange("p (n g d) -> p n g d", g=GROUP, n=KV),
                                      tb[0:R, 0:512].rearrange("p (n g d) -> p n g d", g=GROUP, n=KV), ALU.add)
                    dve.tensor_tensor(rot[0:R, b, 512:960], ta[0:R, 512:960], tb[0:R, 512:960], ALU.add)
                    dve.tensor_tensor(rot[0:R, b, 960:1024], ta[0:R, 896:960], tb[0:R, 896:960], ALU.add).then_inc(rot_ready, 1)


def gated_linear(nc, io, res, sem):
    MID = GC // 2 - 1
    with ExitStack() as ctx:
        def sb(name, shape):
            return ctx.enter_context(nc.sbuf_tensor(name, shape, F32))
        wk = sb("w_gk", [P, 2, 2, KD, P])
        wvr = sb("w_gvr", [P, KD, 512])
        wgf = sb("w_gf", [P, KD, LOWRANK])
        wfa = sb("w_fa_sb", [LOWRANK, GH * GK])
        bfa = sb("b_fa_sb", [P, GH])
        gnorm = sb("gnorm", [P, GH * GK])
        mask = sb("gla_mask_sb", [P, P])
        reset = sb("reset_sb", [P, NT])
        gfT = sb("gfT", [LOWRANK, NT])
        gv = sb("gv", [P, TILES, GH * GK])
        og = sb("og", [P, TILES, GH * GK])
        spare = res["late"][:, 0:4 * NT].rearrange("p (x n) -> p x n", x=4)
        q, k = spare[:, 0, :], spare[:, 1, :]
        factor = [[sb(f"factor{b}_{i}", [P, NT])[:] for i in range(4)] for b in range(2)]
        fa, fb = spare[:, 2, :], spare[:, 3, :]
        dec = sb("dec", [P, 2, NCH])
        zero = sb("zero_state", [P, P])
        at = sb("gla_at", [P, 2, P])
        kl = sb("gla_kl", [P, 2, P])
        S = sb("gla_S", [P, 8, P])
        S0 = sb("gla_S0", [P, GH, P])
        gsil = sb("gsil", [P, 2, GH * GK])
        sq = sb("sq", [P, P])
        ss = sb("ss", [P, TILES, GH])
        pp = ctx.enter_context(nc.psum_tensor("gla_pp", [P, 3, 512], F32))
        pa = ctx.enter_context(nc.psum_tensor("gla_pa", [P, 2, 512], F32))
        po = ctx.enter_context(nc.psum_tensor("gla_po", [P, 512], F32))
        pu = ctx.enter_context(nc.psum_tensor("gla_pu", [P, 2, 512], F32))
        ident, xT = res["ident"], res["xT"]
        x_in, g_in = [sem(f"x_in{kk}") for kk in range(KD)], sem("gla_in")
        v_in, r_in = sem("w_gv_in"), sem("w_gr_in")
        wk_in = [sem("w_gk_in0"), sem("w_gk_in1")]
        gf_ready, gf_copied, gv_ready, gv_copied = sem("gf_ready"), sem("gf_copied"), sem("gv_ready"), sem("gv_copied")
        pre_ready, pre_used, q_ready, q_copied, k_ready, k_copied = (sem(n) for n in
            ("pre_ready", "pre_used", "gq_ready", "gq_copied", "gk_ready", "gk_copied"))
        soft_step, gdiff, gexp, dve_step, factors = (sem(n) for n in ("soft_step", "gdiff", "gexp", "gla_step", "gla_factors"))
        at_ready, at_masked, kl_ready, kl_copied, u_ready, s_next, o_ready, o_copied = (sem(n) for n in
            ("at_ready", "at_masked", "kl_ready", "kl_copied", "u_ready", "s_next", "o_ready", "o_copied"))
        s_out, gr_ready, gr_sig, gr_done, ob_step, ob_ready, obt_ready, obt_copied = (sem(n) for n in
            ("s_out", "gr_ready", "gr_sig", "gr_done", "ob_step", "ob_ready", "obt_ready", "obt_copied"))
        ss_ready, ss_root, u_part = sem("ss_ready"), sem("ss_root"), sem("u_part")
        TC = [(0, 352), (352, 704), (704, 1056)]
        NJ = [r // GC for r in ROWS]
        GROUPS = [(0, SAMPLE, P), (SAMPLE, TILES, TS)]

        with nc.Block() as block:
            @block.sync
            def _(sp):
                wv = io["w_in"].rearrange("(k p) n -> p k n", p=P)
                sp.dma_start(wgf[:], wv[:, :, C_GF:C_GR]).then_inc(x_in[0], 16)
                for kk in range(KD):
                    sp.dma_start(xT[:, kk, :], io["xT"][:, kk, :]).then_inc(x_in[kk], 16)
                for dst, src in ((ident[:], io["ident"]), (wfa[:], io["w_fa"]), (bfa[:], io["b_fa"]),
                                 (gnorm[:], io["g_gla_norm"].to_broadcast([P, GH * GK])),
                                 (mask[:], io["gla_mask"]), (reset[:], io["reset"]),
                                 (S0[:], io["state"].rearrange("h c v -> c h v"))):
                    sp.dma_start(dst, src).then_inc(g_in, 16)
                sp.dma_start(wvr[:], wv[:, :, C_GV:C_GF]).then_inc(v_in, 16)
                for h in range(GH):
                    if h >= 2:
                        sp.wait_ge(k_ready, h - 1)
                    sp.dma_start(wk[:, h % 2, 0, :, :], wv[:, :, C_GQ + h * P:C_GQ + (h + 1) * P]).then_inc(wk_in[h % 2], 16)
                    sp.dma_start(wk[:, h % 2, 1, :, :], wv[:, :, C_GK + h * P:C_GK + (h + 1) * P]).then_inc(wk_in[h % 2], 16)
                sp.wait_ge(gv_ready, TILES)
                sp.dma_start(wvr[:], wv[:, :, C_GR:C_GATE]).then_inc(r_in, 16)

            @block.gpsimd
            def _(pool):
                for h in range(GH):
                    pool.wait_ge(s_next, h * NCH + NCH - 1)
                    pool.dma_start(io["gla_p"][h], S[:, (NCH - 1) % 8, :]).then_inc(s_out, 16)
                    pool.wait_ge(s_next, h * NCH + NCH)
                    pool.dma_start(io["gla_s"][h], S[:, NCH % 8, :]).then_inc(s_out, 16)
                    pool.wait_ge(s_out, 32 * (h + 1))

            @block.tensor
            def _(pe):
                def gates(h):
                    if h:
                        pe.wait_ge(k_copied, h)
                    for c, (a, b) in enumerate(TC):
                        last = pe.matmul(pp[:, c, 0:b - a], wfa[:, h * P:(h + 1) * P], gfT[:, a:b], start=True, stop=True)
                    last.then_inc(pre_ready, 1)

                def third(h, part, c, kk):
                    if (part, c, kk) == (0, 0, 0):
                        pe.wait_ge(wk_in[h % 2], 32 * (h // 2 + 1))
                        pe.wait_ge(pre_used, h + 1)
                        pe.wait_ge(soft_step, 3 * h + 1)
                    if (part, c, kk) == (1, 0, 0):
                        pe.wait_ge(q_copied, h + 1)
                    a, b = TC[c]
                    last = pe.matmul(pp[:, c, 0:b - a], wk[:, h % 2, part, kk, :], xT[:, kk, a:b], start=(kk == 0), stop=(kk == KD - 1))
                    if (c, kk) == (2, KD - 1):
                        last.then_inc(k_ready if part else q_ready, 1)

                def output_gate(t, kk):
                    if kk == 0:
                        if t == 0:
                            pe.wait_ge(r_in, 16)
                            pe.wait_ge(k_copied, GH)
                        if t >= 3:
                            pe.wait_ge(gr_done, t - 2)
                    last = pe.matmul(pp[0:ROWS[t], t % 3, :], xT[:, kk, tok(t)], wvr[:, kk, :], start=(kk == 0), stop=(kk == KD - 1))
                    if kk == KD - 1:
                        last.then_inc(gr_ready, 1)

                def beside(h, t, steps):
                    for kk in steps:
                        if h == GH - 1:
                            output_gate(t, kk)
                        elif t <= 5:
                            third(h + 1, t // 3, t % 3, kk)
                        elif (t, kk) == (7, 0) and h + 2 < GH:
                            gates(h + 2)

                for kk in range(KD):
                    pe.wait_ge(x_in[kk], 16 if kk else 2 * 16)
                    for c, (a, b) in enumerate(TC):
                        last = pe.matmul(pp[0:LOWRANK, c, 0:b - a], wgf[:, kk, :], xT[:, kk, a:b], start=(kk == 0), stop=(kk == KD - 1))
                last.then_inc(gf_ready, 1)
                pe.wait_ge(gf_copied, 1)
                pe.wait_ge(g_in, 7 * 16)
                gates(0)
                pe.wait_ge(v_in, 16)
                for t in range(TILES):
                    if t >= 2:
                        pe.wait_ge(gv_copied, t - 1)
                    for kk in range(KD):
                        last = pe.matmul(pa[0:ROWS[t], t % 2, :], xT[:, kk, tok(t)], wvr[:, kk, :], start=(kk == 0), stop=(kk == KD - 1))
                    last.then_inc(gv_ready, 1)
                for part in range(2):
                    for c in range(3):
                        for kk in range(KD):
                            third(0, part, c, kk)
                gates(1)
                pe.wait_ge(gv_copied, TILES)
                for h in range(GH):
                    pe.wait_ge(factors, h + 1)
                    for t in range(TILES):
                        n, R = h * TILES + t, ROWS[t]
                        s = tok(t)
                        if n >= 1:
                            pe.wait_ge(at_masked, n)
                            pe.wait_ge(kl_copied, n)
                        f = factor[h % 2]
                        pe.transpose(pa[0:R, 1, 0:P], f[3][:, s], ident[:]).then_inc(kl_ready, 1)
                        pe.matmul(pa[0:R, 0, 0:R], f[1][:, s], f[0][:, s], start=True, stop=True).then_inc(at_ready, 1)
                        beside(h, t, (0, 1))
                        pe.wait_ge(kl_copied, n + 1)
                        if n >= 2:
                            m = n - 2
                            pe.wait_ge(s_next, (m // TILES) * NCH + sum(NJ[:m % TILES + 1]))
                        for j in range(NJ[t]):
                            if j:
                                pe.wait_ge(u_part, h * 3 * SAMPLE + 3 * t + j)
                            last = pe.matmul(pu[:, n % 2, j * P:(j + 1) * P], kl[GC * j:GC * (j + 1), n % 2, :],
                                             gv[GC * j:GC * (j + 1), t, h * P:(h + 1) * P], start=True, stop=True)
                            last.then_inc(u_part if j < NJ[t] - 1 else u_ready, 1)
                            if j < 3:
                                beside(h, t, (2 + j,) if NJ[t] > 1 else (2, 3, 4, 5, 6, 7))
                        pe.wait_ge(at_masked, n + 1)
                        if n >= 1:
                            pe.wait_ge(o_copied, n)
                        pe.matmul(po[0:R, 0:P], at[0:R, n % 2, 0:R], gv[0:R, t, h * P:(h + 1) * P], start=True, stop=False)
                        for j in range(NJ[t]):
                            i = t * (P // GC) + j
                            if j:
                                beside(h, t, (4 + j,))
                            if t < SAMPLE:
                                if i:
                                    pe.wait_ge(s_next, h * NCH + i)
                            st = S0[:, h, :] if t == SAMPLE else S[:, i % 8, :] if i else zero[:]
                            last = pe.matmul(po[GC * j:GC * (j + 1), 0:P], f[2][:, i * GC:(i + 1) * GC], st,
                                             start=False, stop=True)
                        last.then_inc(o_ready, 1)
                for t in range(TILES):
                    R = ROWS[t]
                    pe.wait_ge(ob_ready, t + 1)
                    pe.wait_ge(s_next, GH * NCH)
                    if t >= 2:
                        pe.wait_ge(obt_copied, t - 1)
                    for b in range(4):
                        last = pe.transpose(pu[:, t % 2, b * P:b * P + R], og[0:R, t, b * P:(b + 1) * P], ident[0:R, 0:R])
                    last.then_inc(obt_ready, 1)

            @block.scalar
            def _(act):
                def whole(x):
                    return x.rearrange("p (c n) -> p c n", c=3)

                def softplus(h):
                    if h:
                        act.wait_ge(gexp, h)
                    act.wait_ge(pre_ready, h + 1)
                    act.activation(whole(fa), pp[:, :, 0:352], ACT.Abs, bias=bfa[:, h:h + 1]).then_inc(soft_step, 1)
                    act.wait_ge(soft_step, 3 * h + 1)
                    act.activation(fa, fa, ACT.Exp, scale=-1.0).then_inc(soft_step, 1)
                    act.wait_ge(soft_step, 3 * h + 2)
                    act.activation(fa, fa, ACT.Ln, bias=1.0).then_inc(soft_step, 1)

                def copy_q(h):
                    act.wait_ge(q_ready, h + 1)
                    if h:
                        act.wait_ge(factors, h)
                    act.mul(whole(q), pp[:, :, 0:352], GK ** -0.5).then_inc(q_copied, 1)

                def copy_k(h):
                    act.wait_ge(k_ready, h + 1)
                    act.copy(whole(k), pp[:, :, 0:352]).then_inc(k_copied, 1)

                def decays(h):
                    f = factor[h % 2]
                    act.wait_ge(gdiff, h + 1)
                    if h >= 2:
                        act.wait_ge(o_ready, (h - 1) * TILES)
                    act.activation(f[0], fa, ACT.Exp, scale=1.0 / TAU)
                    act.activation(f[1], fa, ACT.Exp, scale=-1.0 / TAU)
                    act.activation(f[2], fb, ACT.Exp, scale=1.0 / TAU)
                    act.activation(f[3], f[3], ACT.Exp, scale=1.0 / TAU)
                    act.activation(dec[:, h % 2, :].unsqueeze(2), fb.rearrange("p (c n) -> p c n", n=GC)[:, :, GC - 1:GC],
                                   ACT.Exp, scale=1.0 / TAU).then_inc(gexp, 1)

                def beside(h, t):
                    if h == GH - 1:
                        act.wait_ge(gr_ready, t + 1)
                        if t >= 2:
                            act.wait_ge(gr_done, t - 1)
                            act.wait_ge(ob_step, t - 1)
                        act.activation(gsil[0:ROWS[t], t % 2, :], pp[0:ROWS[t], t % 3, :], ACT.Sigmoid).then_inc(gr_sig, 1)
                    elif t == 0:
                        decays(h + 1)
                    elif t == 2:
                        copy_q(h + 1)
                    elif t == 5:
                        copy_k(h + 1)
                    elif t == 7 and h + 2 < GH:
                        softplus(h + 2)

                act.wait_ge(gf_ready, 1)
                for c, (a, b) in enumerate(TC):
                    last = act.copy(gfT[:, a:b], pp[0:LOWRANK, c, 0:b - a])
                last.then_inc(gf_copied, 1)
                act.wait_ge(g_in, 7 * 16)
                softplus(0)
                decays(0)
                for t in range(TILES):
                    act.wait_ge(gv_ready, t + 1)
                    act.copy(gv[0:ROWS[t], t, :], pa[0:ROWS[t], t % 2, :]).then_inc(gv_copied, 1)
                copy_q(0)
                copy_k(0)
                softplus(1)
                for h in range(GH):
                    for t in range(TILES):
                        n, R = h * TILES + t, ROWS[t]
                        act.wait_ge(kl_ready, n + 1)
                        if n >= 2:
                            act.wait_ge(u_ready, n - 1)
                        act.copy(kl[0:R, n % 2, :], pa[0:R, 1, 0:P]).then_inc(kl_copied, 1)
                        act.wait_ge(o_ready, n + 1)
                        act.copy(og[0:R, t, h * P:(h + 1) * P], po[0:R, 0:P]).then_inc(o_copied, 1)
                        beside(h, t)
                for a, b, R in GROUPS:
                    act.wait_ge(ss_ready, 1)
                    last = act.activation(ss[0:R, a:b, :], ss[0:R, a:b, :], ACT.Sqrt)
                last.then_inc(ss_root, 1)
                for t in range(TILES):
                    R = ROWS[t]
                    act.wait_ge(obt_ready, t + 1)
                    act.copy(res["obT"][:, :, tok(t)], pu[:, t % 2, :].rearrange("p (b r) -> p b r", b=4)[:, :, 0:R]).then_inc(obt_copied, 1)

            @block.vector
            def _(dve):
                link = Link(dve, dve_step)

                def chunks(x):
                    return x.rearrange("p (c n) -> p c n", n=GC)

                def cut_gates(h):
                    dve.wait_ge(pre_ready, h + 1)
                    if h:
                        dve.wait_ge(gexp, h)
                    link.wait()
                    dve.wait_ge(soft_step, 3 * h + 1)
                    dve.tensor_scalar(fb.rearrange("p (c n) -> p c n", c=3), pp[:, :, 0:352], bfa[:, h:h + 1], 0.0,
                                      ALU.add, ALU.min).then_inc(pre_used, 1)

                def sum_gates(h):
                    dve.wait_ge(pre_used, h + 1)
                    dve.wait_ge(soft_step, 3 * h + 3)
                    link.add(dve.tensor_tensor(fa, fb, fa, ALU.subtract))
                    link.wait()
                    link.add(dve.tensor_tensor_scan(fb, reset[:], fa, 0.0, ALU.mult, ALU.add))
                    link.wait()
                    b3 = chunks(fb)
                    link.add(dve.tensor_tensor(chunks(fa), b3, b3[:, :, MID:MID + 1].to_broadcast([P, NCH, GC]), ALU.subtract))

                def gates_left(h):
                    link.wait()
                    b3 = chunks(fb)
                    if h >= 2:
                        dve.wait_ge(o_ready, (h - 1) * TILES)
                    dve.tensor_tensor(chunks(factor[h % 2][3]), b3[:, :, GC - 1:GC].to_broadcast([P, NCH, GC]), b3,
                                      ALU.subtract).then_inc(gdiff, 1)

                def factors_of(h):
                    f = factor[h % 2]
                    dve.wait_ge(gexp, h + 1)
                    dve.wait_ge(q_copied, h + 1)
                    dve.wait_ge(k_copied, h + 1)
                    dve.tensor_tensor(f[0], f[0], q, ALU.mult)
                    dve.tensor_tensor(f[1], f[1], k, ALU.mult)
                    dve.tensor_tensor(f[2], f[2], q, ALU.mult)
                    dve.tensor_tensor(f[3], f[3], k, ALU.mult).then_inc(factors, 1)

                def gate_tile(t):
                    R = ROWS[t]
                    dve.wait_ge(o_copied, (GH - 1) * TILES + t + 1)
                    for h in range(GH):
                        o = og[0:R, t, h * P:(h + 1) * P]
                        link.wait()
                        link.add(dve.tensor_tensor_reduce(sq[0:R, :], o, o, 1.0 / P, 0.0, ALU.mult, ALU.add, ss[0:R, t, h:h + 1]))
                    dve.wait_ge(gr_sig, t + 1)
                    link.add(dve.tensor_tensor(gsil[0:R, t % 2, :], gsil[0:R, t % 2, :], gnorm[0:R, :], ALU.mult))
                    link.wait()
                    dve.tensor_tensor(gsil[0:R, t % 2, :], gsil[0:R, t % 2, :], pp[0:R, t % 3, :], ALU.mult).then_inc(gr_done, 1)
                    dve.wait_ge(gr_done, t + 1)
                    dve.tensor_tensor(og[0:R, t, :], og[0:R, t, :], gsil[0:R, t % 2, :], ALU.mult).then_inc(ob_step, 1)

                def beside(h, t):
                    if h == GH - 1:
                        if t:
                            gate_tile(t - 1)
                    elif t == 0:
                        gates_left(h + 1)
                    elif t == 6:
                        factors_of(h + 1)
                    elif t == 7 and h + 2 < GH:
                        cut_gates(h + 2)
                    elif t == 8 and h + 2 < GH:
                        sum_gates(h + 2)

                dve.wait_ge(g_in, 7 * 16)
                link.add(dve.memset(zero[:], 0.0))
                cut_gates(0)
                sum_gates(0)
                gates_left(0)
                factors_of(0)
                cut_gates(1)
                sum_gates(1)
                dve.wait_ge(factors, 1)
                for h in range(GH):
                    for t in range(TILES):
                        n, R = h * TILES + t, ROWS[t]
                        dve.wait_ge(at_ready, n + 1)
                        if n >= 2:
                            dve.wait_ge(o_ready, n - 1)
                        dve.tensor_tensor(at[0:R, n % 2, 0:R], pa[0:R, 0, 0:R], mask[0:R, 0:R], ALU.mult).then_inc(at_masked, 1)
                        dve.wait_ge(u_ready, n + 1)
                        for j in range(NJ[t]):
                            i = t * (P // GC) + j
                            src = S0[:, h, :] if t == SAMPLE else S[:, i % 8, :] if i else zero[:]
                            if i or h:
                                dve.wait_ge(s_next, h * NCH + i)
                            if i == 0 and h:
                                dve.wait_ge(s_out, 32 * h)
                                dve.wait_ge(o_ready, h * TILES)
                            dve.scalar_tensor_tensor(S[:, (i + 1) % 8, :], src, dec[:, h % 2, i:i + 1], pu[:, n % 2, j * P:(j + 1) * P],
                                                     ALU.mult, ALU.add).then_inc(s_next, 1)
                        beside(h, t)
                gate_tile(SAMPLE)
                link.wait()
                for a, b, R in GROUPS:
                    last = dve.tensor_scalar(ss[0:R, a:b, :], ss[0:R, a:b, :], EPS, None, ALU.add)
                last.then_inc(ss_ready, 1)
                dve.wait_ge(ss_root, 1)
                for a, b, R in GROUPS:
                    link.add(dve.reciprocal(ss[0:R, a:b, :], ss[0:R, a:b, :]))
                link.wait()
                dve.wait_ge(ob_step, TILES)
                for t in range(TILES):
                    R = ROWS[t]
                    o = og[0:R, t, :].rearrange("p (h d) -> p h d", h=GH)
                    dve.tensor_tensor(o, o, ss[0:R, t, :].unsqueeze(2).to_broadcast([R, GH, P]), ALU.mult).then_inc(ob_ready, 1)


def sparse_attention(nc, io, res, sem):
    with ExitStack() as ctx:
        def sb(name, shape):
            return ctx.enter_context(nc.sbuf_tensor(name, shape, F32))
        rl = sb("relu", [P, 2, TP])
        score = sb("score", [P, 2, TP])
        bias = sb("bias", [P, TP])
        wb = sb("w_b", [P, 2, 12, P])
        sg = res["tail"][:, 0:352]
        m8 = sb("m8", [P, 2, 8])
        lg = sb("logits", [P, 2, TP])
        pr = sb("probs", [P, 2, TP])
        prT = sb("probsT", [P, 2, TP])
        mx = sb("mx", [P, HEADS])
        nmx = sb("nmx", [P, HEADS])
        sm = sb("sm", [P, 2, HEADS])
        rs = sb("rs", [P, HEADS])
        oa = sb("oa", [P, 2, 512])
        ps = ctx.enter_context(nc.psum_tensor("att_ps", [P, 2, TP], F32))
        pt = ctx.enter_context(nc.psum_tensor("att_pt", [P, TP], F32))
        po = ctx.enter_context(nc.psum_tensor("att_po", [P, 512], F32))
        pg = ctx.enter_context(nc.psum_tensor("att_pg", [P, 512], F32))
        ident, xT = res["ident"], res["xT"]
        (is_ready, relu_done, sc_step, round_step, sel_ready, lg_ready, lg_done, mx_done, p_ready, pt_ready, pt_copied, o_ready,
         oa_ready, oat_ready, oat_copied) = (sem(n) for n in (
            "is_ready", "relu_done", "sc_step", "round_step", "sel_ready", "lg_ready", "lg_done", "mx_done", "p_ready",
            "pt_ready", "pt_copied", "att_o_ready", "oa_ready", "oat_ready", "oat_copied"))
        gb_ready, gb_sig, yb_ready, mb_ready = sem("gb_ready"), sem("gb_sig"), sem("yb_ready"), sem("mb_ready")
        wb_in = [sem("w_b_in0"), sem("w_b_in1")]
        TC = [(0, 352), (352, 704), (704, 1056)]

        def mix_beside(t, h):
            return divmod((t - 1) * HEADS + h, 2) if 1 <= t <= 6 else None
        assert 6 * HEADS == 2 * 3 * KD
        LEN = [(t + 1) * P for t in range(SAMPLE)] + [PAST + TS]
        NEED = [TOPK_P] * SAMPLE + [TOPK_S]
        CHOOSE = [t for t in range(TILES) if LEN[t] > NEED[t]]

        def keys(t):
            return [(a, min(a + 512, LEN[t])) for a in range(0, LEN[t], 512)]

        def kchunks(t):
            return [(a, min(a + P, LEN[t])) for a in range(0, LEN[t], P)]

        def index_beside(t, h):
            return (t + 2, h - (HEADS - IH)) if h >= HEADS - IH and t + 2 in CHOOSE else None

        order = []
        for t in range(TILES):
            for h in range(HEADS):
                order.append((t, "logit", h))
                if index_beside(t, h):
                    order.append((index_beside(t, h)[0], "index", index_beside(t, h)[1]))
        slot = {key: n for n, key in enumerate(order)}

        def seen(key):
            return sum(1 for x in order[:slot[key] + 1] if x[1] == key[1])

        with nc.Block() as block:
            @block.sync
            def _(sp):
                wv = io["w_in"].rearrange("(k p) n -> p k n", p=P)
                pbv = io["w_pb"].rearrange("(k p) n -> p k n", p=P)
                for f in range(KD):
                    if f >= 2:
                        sp.wait_ge(yb_ready, 3 * (f - 1))
                    sp.dma_start(wb[:, f % 2, 0:8, :], wv[:, :, C_GATE + D + f * P:C_GATE + D + (f + 1) * P]).then_inc(wb_in[f % 2], 16)
                    sp.dma_start(wb[:, f % 2, 8:12, :], pbv[:, :, f * P:(f + 1) * P]).then_inc(wb_in[f % 2], 16)

            @block.tensor
            def _(pe):
                def mix_product(n, which):
                    f, (a, b) = n // 3, TC[n % 3]
                    if which == 0:
                        pe.wait_ge(wb_in[f % 2], 32 * (f // 2 + 1))
                        if n:
                            pe.wait_ge(mb_ready, n)
                    else:
                        pe.wait_ge(gb_sig, n + 1)
                    lo, kn, rhs = ((0, 8, xT), (8, 4, res["obT"]))[which]
                    for kk in range(kn):
                        last = pe.matmul(pg[:, 0:b - a], wb[:, f % 2, lo + kk, :], rhs[:, kk, a:b], start=(kk == 0), stop=(kk == kn - 1))
                    last.then_inc(yb_ready if which else gb_ready, 1)

                def free(n):
                    if n >= 2:
                        key = order[n - 2]
                        pe.wait_ge(relu_done if key[1] == "index" else lg_done, seen(key))

                def scores(t, kind, h):
                    n, R = slot[(t, kind, h)], ROWS[t]
                    free(n)
                    if kind == "index":
                        base, l, kT = HD * (h % 2), res["iqT"][:, h // 2, tok(t)], res["ikT"] if t < SAMPLE else res["ikTs"]
                    else:
                        base, l, kT = HD * (h // GROUP), res["aqT"][:, h % GROUP, tok(t)], res["kT"] if t < SAMPLE else res["kTs"]
                    for a, b in keys(t):
                        last = pe.matmul(ps[0:R, n % 2, a:b], l[base:base + HD, :], kT[base:base + HD, a:b], start=True, stop=True)
                    last.then_inc(is_ready if kind == "index" else lg_ready, 1)

                def transposes(t, h):
                    R, m = ROWS[t], t * HEADS + h
                    pe.wait_ge(p_ready, m + 1)
                    if m >= 1:
                        pe.wait_ge(pt_copied, m)
                    if h == 1 and t >= 1:
                        pe.wait_ge(oat_copied, t)
                    for c, (a, b) in enumerate(kchunks(t)):
                        last = pe.transpose(pt[0:b - a, c * P:c * P + R], pr[0:R, m % 2, a:b], ident[0:R, 0:R])
                    last.then_inc(pt_ready, 1)

                def values(t, h):
                    R, m = ROWS[t], t * HEADS + h
                    pe.wait_ge(pt_copied, m + 1)
                    if h == 0 and t >= 1:
                        pe.wait_ge(oa_ready, t)
                    V = res["V"] if t < SAMPLE else res["Vs"]
                    ch = kchunks(t)
                    for c, (a, b) in enumerate(ch):
                        last = pe.matmul(po[0:R, h * HD:(h + 1) * HD], prT[0:b - a, m % 2, c * P:c * P + R],
                                         V[0:b - a, c, (h // GROUP) * HD:(h // GROUP + 1) * HD], start=(c == 0), stop=(c == len(ch) - 1))
                    last.then_inc(o_ready, 1)

                def next_scores(t, h):
                    scores(t, "logit", h)
                    if index_beside(t, h):
                        scores(index_beside(t, h)[0], "index", index_beside(t, h)[1])

                def finish(t):
                    R = ROWS[t]
                    pe.wait_ge(oa_ready, t + 1)
                    for b in range(4):
                        last = pe.transpose(pt[:, b * P:b * P + R], oa[0:R, t % 2, b * P:(b + 1) * P], ident[0:R, 0:R])
                    last.then_inc(oat_ready, 1)

                next_scores(0, 0)
                for t in range(TILES):
                    for h in range(HEADS):
                        before = (t, h - 1) if h else (t - 1, HEADS - 1)
                        if t or h:
                            transposes(*before)
                        if h < HEADS - 1:
                            next_scores(t, h + 1)
                        elif t < SAMPLE:
                            next_scores(t + 1, 0)
                        if mix_beside(t, h):
                            mix_product(*mix_beside(t, h))
                        if t or h:
                            values(*before)
                        if h == 1 and t:
                            finish(t - 1)
                transposes(SAMPLE, HEADS - 1)
                values(SAMPLE, HEADS - 1)
                finish(SAMPLE)

            @block.scalar
            def _(act):
                def probs(t, h):
                    R, m, L = ROWS[t], t * HEADS + h, LEN[t]
                    act.wait_ge(mx_done, m + 1)
                    if m >= 2:
                        act.wait_ge(pt_ready, m - 1)
                    act.activation(pr[0:R, m % 2, 0:L], lg[0:R, m % 2, 0:L], ACT.Exp, bias=nmx[0:R, h:h + 1], scale=HD ** -0.5,
                                   accum_out=sm[0:R, t % 2, h:h + 1]).then_inc(p_ready, 1)

                def turned(t, h):
                    R, m = ROWS[t], t * HEADS + h
                    act.wait_ge(pt_ready, m + 1)
                    if m >= 2:
                        act.wait_ge(o_ready, m - 1)
                    ch = kchunks(t)
                    full = [c for c, (a, b) in enumerate(ch) if b - a == P]
                    v = pt[:].rearrange("p (c r) -> p c r", r=P)
                    d = prT[:, m % 2, :].rearrange("p (c r) -> p c r", r=P)
                    last = act.copy(d[:, 0:len(full), 0:R], v[:, 0:len(full), 0:R])
                    if len(full) < len(ch):
                        k = ch[-1][1] - ch[-1][0]
                        last = act.copy(d[0:k, len(full), 0:R], v[0:k, len(full), 0:R])
                    last.then_inc(pt_copied, 1)

                def finish(t):
                    act.wait_ge(oat_ready, t + 1)
                    act.copy(res["oaT"][:, :, tok(t)], pt[:, 0:512].rearrange("p (b r) -> p b r", b=4)[:, :, 0:ROWS[t]]).then_inc(oat_copied, 1)

                nrelu = 0
                for t in range(TILES):
                    for h in range(HEADS):
                        probs(t, h)
                        if index_beside(t, h):
                            tile, head = index_beside(t, h)
                            R, L = ROWS[tile], LEN[tile]
                            act.wait_ge(is_ready, nrelu + 1)
                            if nrelu >= 2:
                                act.wait_ge(sc_step, nrelu - 1)
                            act.activation(rl[0:R, nrelu % 2, 0:L], ps[0:R, slot[(tile, "index", head)] % 2, 0:L], ACT.Relu).then_inc(relu_done, 1)
                            nrelu += 1
                        if h:
                            turned(t, h - 1)
                        elif t:
                            turned(t - 1, HEADS - 1)
                        if h == 1 and t:
                            finish(t - 1)
                        if mix_beside(t, h):
                            n, which = mix_beside(t, h)
                            if which == 0:
                                act.wait_ge(gb_ready, n + 1)
                                if n:
                                    act.wait_ge(mb_ready, n)
                                act.activation(sg, pg[:, 0:352], ACT.Sigmoid).then_inc(gb_sig, 1)
                turned(SAMPLE, HEADS - 1)
                finish(SAMPLE)

            @block.vector
            def _(dve):
                link = Link(dve, round_step)
                summed = 0

                def score_sum(t, h):
                    nonlocal summed
                    R, L = ROWS[t], LEN[t]
                    s = score[0:R, t % 2, :]
                    dve.wait_ge(relu_done, summed + 1)
                    link.wait()
                    if h:
                        dve.wait_ge(sc_step, summed)
                    w = res["iw"][0:R, t, h:h + 1]
                    r = rl[0:R, summed % 2, 0:L]
                    if h == 0:
                        ins = dve.tensor_scalar(s[:, 0:L], r, w, None, ALU.mult)
                    else:
                        ins = dve.scalar_tensor_tensor(s[:, 0:L], r, w, s[:, 0:L], ALU.mult, ALU.add)
                    ins.then_inc(sc_step, 1)
                    summed += 1
                    if h == IH - 1:
                        dve.wait_ge(sc_step, summed)
                        if t < SAMPLE:
                            link.add(dve.memset(score[0:CHUNK, t % 2, L - CHUNK:L], GONE))
                            link.wait()

                def finish(t):
                    R = ROWS[t]
                    dve.wait_ge(p_ready, (t + 1) * HEADS)
                    link.wait()
                    link.add(dve.reciprocal(rs[0:R, :], sm[0:R, t % 2, :]))
                    link.wait()
                    dve.wait_ge(o_ready, (t + 1) * HEADS)
                    if t >= 2:
                        dve.wait_ge(oat_ready, t - 1)
                    if t >= 1:
                        dve.wait_ge(oa_ready, t)
                    dve.tensor_tensor(oa[0:R, t % 2, :].rearrange("p (h d) -> p h d", d=HD), po[0:R, :].rearrange("p (h d) -> p h d", d=HD),
                                      rs[0:R, :].unsqueeze(2).to_broadcast([R, HEADS, HD]), ALU.mult).then_inc(oa_ready, 1)
                    dve.wait_ge(oa_ready, t + 1)

                def rounds(t, part):
                    R, n = ROWS[t], NEED[t] // 8
                    s = score[0:R, t % 2, 0:LEN[t]]
                    for r in range(n * part // HEADS, n * (part + 1) // HEADS):
                        link.add(dve.max(m8[0:R, r % 2, :], s))
                        link.wait()
                        link.add(dve.match_replace(s, m8[0:R, r % 2, :], s, GONE))
                        link.wait()

                for t in range(TILES):
                    R, L = ROWS[t], LEN[t]
                    bv = bias[0:R, :]
                    if t:
                        dve.wait_ge(lg_done, t * HEADS)
                    if t in CHOOSE:
                        link.add(dve.tensor_scalar(bv[:, 0:L], score[0:R, t % 2, 0:L], GONE, -1.0e30, ALU.is_gt, ALU.mult))
                    else:
                        link.add(dve.memset(bv[:, 0:L], 0.0))
                    link.wait()
                    if t < SAMPLE:
                        link.add(dve.memset(bias[0:CHUNK, L - CHUNK:L], -1.0e30))
                        link.wait()
                    for h in range(HEADS):
                        m = t * HEADS + h
                        dve.wait_ge(lg_ready, m + 1)
                        if m >= 2:
                            dve.wait_ge(p_ready, m - 1)
                        dve.tensor_tensor_reduce(lg[0:R, m % 2, 0:L], ps[0:R, slot[(t, "logit", h)] % 2, 0:L], bv[:, 0:L], 1.0, -1.0e38,
                                                 ALU.add, ALU.max, mx[0:R, h:h + 1]).then_inc(lg_done, 1)
                        dve.wait_ge(lg_done, m + 1)
                        if t >= 1:
                            dve.wait_ge(p_ready, m - HEADS + 1)
                        dve.tensor_scalar(nmx[0:R, h:h + 1], mx[0:R, h:h + 1], -HD ** -0.5, None, ALU.mult).then_inc(mx_done, 1)
                        if t and mix_beside(*((t, h - 1) if h else (t - 1, HEADS - 1))):
                            n, which = mix_beside(*((t, h - 1) if h else (t - 1, HEADS - 1)))
                            if which == 1:
                                f, (a, b) = n // 3, TC[n % 3]
                                dve.wait_ge(yb_ready, n + 1)
                                dve.tensor_tensor(res["mT"][:, f, a:b], sg, pg[:, 0:352], ALU.mult).then_inc(mb_ready, 1)
                        if t + 1 in CHOOSE:
                            rounds(t + 1, h)
                        if h == 0 and t:
                            finish(t - 1)
                        if index_beside(t, h):
                            score_sum(*index_beside(t, h))
                finish(SAMPLE)


def layer_norm(dve, link, x, st, mv, gain, offset, R, root_asked, root_given, nth):
    for c in range(2):
        link.add(dve.bn_stats(st[0:R, c * 6:c * 6 + 6], x[:, c * 512:(c + 1) * 512]))
    link.wait()
    link.add(dve.bn_aggr(mv[0:R, 0:2], st[0:R, :]))
    link.wait()
    dve.tensor_scalar(mv[0:R, 1:2], mv[0:R, 1:2], EPS, None, ALU.add).then_inc(root_asked, 1)
    dve.wait_ge(root_given, nth + 1)
    link.add(dve.reciprocal(mv[0:R, 1:2], mv[0:R, 1:2]))
    link.wait()
    link.add(dve.tensor_scalar(x, x, mv[0:R, 0:1], mv[0:R, 1:2], ALU.subtract, ALU.mult))
    link.wait()
    link.add(dve.tensor_tensor(x, x, gain[0:R, :], ALU.mult))
    link.wait()
    return dve.tensor_tensor(x, x, offset[0:R, :], ALU.add)


def merge(nc, io, res, sem):
    with ExitStack() as ctx:
        def sb(name, shape):
            return ctx.enter_context(nc.sbuf_tensor(name, shape, F32))
        wb = sb("w_merge", [P, 2, 12, P])
        wo = sb("w_out_sb", [P, KD, D])
        mT = res["mT"]
        sg = sb("sig", [P, 2, 352])
        pr = sb("gated", [P, 352])
        xt = sb("x_tok", [P, 2, D])
        gain, offset = sb("ln1_g_sb", [P, D]), sb("ln1_b_sb", [P, D])
        st, mv = sb("ln1_st", [P, 12]), sb("ln1_mv", [P, 2])
        pm = ctx.enter_context(nc.psum_tensor("mg_pm", [P, 8, 512], F32))
        ident, xT = res["ident"], res["xT"]
        (ln_in, wo_in, g_ready, sig_done, g_step, m_ready, mix_ready, mix_used, ln_step, root_asked,
         root_given, h_ready, ht_ready, ht_copied) = (sem(n) for n in (
            "ln1_in", "w_out_in", "g_ready", "sig_done", "g_step", "m_ready", "mix_ready", "mix_used",
            "ln1_step", "root1_asked", "root1_given", "h1_ready", "h1t_ready", "h1t_copied"))
        wb_in = [sem("w_merge_in0"), sem("w_merge_in1")]
        xt_in = [sem("x_tok_in0"), sem("x_tok_in1")]
        TC = [(0, 352), (352, 704), (704, 1056)]

        with nc.Block() as block:
            @block.sync
            def _(sp):
                wv = io["w_in"].rearrange("(k p) n -> p k n", p=P)
                pav = io["w_pa"].rearrange("(k p) n -> p k n", p=P)
                for f in range(KD):
                    if f >= 2:
                        sp.wait_ge(g_ready, 3 * (f - 1))
                    for lo, n, src, c in ((0, 8, wv, C_GATE), (8, 4, pav, 0)):
                        sp.dma_start(wb[:, f % 2, lo:lo + n, :], src[:, :, c + f * P:c + (f + 1) * P]).then_inc(wb_in[f % 2], 16)
                    if f == 1:
                        sp.dma_start(gain[:], io["ln1_g"].to_broadcast([P, D])).then_inc(ln_in, 16)
                        sp.dma_start(offset[:], io["ln1_b"].to_broadcast([P, D])).then_inc(ln_in, 16)
                        sp.dma_start(wo[:], io["w_out"].rearrange("(k p) n -> p k n", p=P)).then_inc(wo_in, 16)
                for t in range(TILES):
                    R = ROWS[t]
                    if t >= 2:
                        sp.wait_ge(mix_used, t - 1)
                    src = io["x_p"][t * P:(t + 1) * P, :] if t < SAMPLE else io["x_s"]
                    sp.dma_start(xt[0:R, t % 2, :], src).then_inc(xt_in[t % 2], 16)

            @block.tensor
            def _(pe):
                for f in range(KD):
                    pe.wait_ge(wb_in[f % 2], 32 * (f // 2 + 1))
                    for c, (a, b) in enumerate(TC):
                        n = f * 3 + c
                        bank = 4 * (n % 2)
                        if n >= 2:
                            pe.wait_ge(m_ready, n - 1)
                        for g, lo, kn, rhs in ((0, 0, 8, xT), (2, 8, 4, res["oaT"])):
                            for kk in range(kn):
                                last = pe.matmul(pm[:, bank + g, 0:b - a], wb[:, f % 2, lo + kk, :], rhs[:, kk, a:b],
                                                 start=(kk == 0), stop=(kk == kn - 1))
                        last.then_inc(g_ready, 1)
                pe.wait_ge(m_ready, 3 * KD)
                pe.wait_ge(wo_in, 16)

                def transposes(t):
                    R = ROWS[t]
                    pe.wait_ge(h_ready, t + 1)
                    if t >= 1:
                        pe.wait_ge(ht_copied, t)
                    for kk in range(KD):
                        last = pe.transpose(pm[:, 4 + kk // 4, (kk % 4) * P:(kk % 4) * P + R], res["h1"][0:R, t, kk * P:(kk + 1) * P], ident[0:R, 0:R])
                    last.then_inc(ht_ready, 1)

                for t in range(TILES):
                    R = ROWS[t]
                    if t >= 2:
                        pe.wait_ge(mix_used, t - 1)
                    for c in range(2):
                        for kk in range(KD):
                            last = pe.matmul(pm[0:R, 2 * (t % 2) + c, :], mT[:, kk, tok(t)], wo[:, kk, c * 512:(c + 1) * 512],
                                             start=(kk == 0), stop=(kk == KD - 1))
                    last.then_inc(mix_ready, 1)
                    if t >= 1:
                        transposes(t - 1)
                transposes(SAMPLE)

            @block.scalar
            def _(act):
                for n in range(3 * KD):
                    act.wait_ge(g_ready, n + 1)
                    if n >= 2:
                        act.wait_ge(m_ready, n - 1)
                    act.activation(sg[:, n % 2, :], pm[:, 4 * (n % 2), 0:352], ACT.Sigmoid).then_inc(sig_done, 1)

                def copies(t):
                    R = ROWS[t]
                    act.wait_ge(ht_ready, t + 1)
                    act.copy(res["h1T"][:, :, tok(t)], pm[:, 4:6, :].rearrange("p a (b r) -> p (a b) r", r=P)[:, :, 0:R]).then_inc(ht_copied, 1)

                for t in range(TILES):
                    R = ROWS[t]
                    act.wait_ge(root_asked, t + 1)
                    act.activation(mv[0:R, 1:2], mv[0:R, 1:2], ACT.Sqrt).then_inc(root_given, 1)
                    if t >= 1:
                        copies(t - 1)
                copies(SAMPLE)

            @block.vector
            def _(dve):
                link = Link(dve, g_step)
                for n in range(3 * KD):
                    f, (a, b) = n // 3, TC[n % 3]
                    bank = 4 * (n % 2)
                    dve.wait_ge(sig_done, n + 1)
                    if n >= 1:
                        dve.wait_ge(m_ready, n)
                    link.add(dve.tensor_tensor(pr[:, :], sg[:, n % 2, :], pm[:, bank + 2, 0:352], ALU.mult))
                    link.wait()
                    dve.tensor_tensor(mT[:, f, a:b], mT[:, f, a:b], pr[:, :], ALU.add).then_inc(m_ready, 1)
                dve.wait_ge(ln_in, 32)
                for t in range(TILES):
                    R = ROWS[t]
                    x = res["h1"][0:R, t, :]
                    dve.wait_ge(mix_ready, t + 1)
                    dve.wait_ge(xt_in[t % 2], 16 * (t // 2 + 1))
                    dve.scalar_tensor_tensor(x, xt[0:R, t % 2, :], ALPHA, pm[0:R, 2 * (t % 2):2 * (t % 2) + 2, :].rearrange("p a b -> p (a b)"),
                                             ALU.mult, ALU.add).then_inc(mix_used, 1)
                    dve.wait_ge(mix_used, t + 1)
                    if t >= 1:
                        dve.wait_ge(h_ready, t)
                    layer_norm(dve, link, x, st, mv, gain, offset, R, root_asked, root_given, t).then_inc(h_ready, 1)


def run_experts(nc, io, res, sem):
    RING = 8
    DG = 4
    MAIN = TILES - 1
    GROUPS = [[0, 1], [2, 3, 4, 5], [6, 7, 8]]
    NB = 2 * PH
    NS = PH * PK * TS // P
    with ExitStack() as ctx:
        def sb(name, shape, dt=F32):
            return ctx.enter_context(nc.sbuf_tensor(name, shape, dt))
        wq = sb("w_pq_sb", [P, 2, KD, P])
        pk = sb("pk_sb", [P, NB, P])
        qT = sb("pqT", [P, 2, 4 * P])
        kw = sb("key_scores", [P, 2, 4, P])
        v = sb("key_top", [P, 4, NB, PK])
        iu = sb("key_at", [P, 4, NB, PK], U32)
        fi = sb("key_at_f", [P, NB, PK])
        cand = sb("cand", [P, PH, NCAND])
        cidx = sb("cand_e", [P, PH, NCAND])
        top = sb("top", [P, PH, PK])
        tat = sb("top_at", [P, PH, PK], U32)
        taf = sb("top_at_f", [P, PH, PK])
        ef = sb("expert_f", [P, PH, PK])
        hot = sb("one_hot", [P, PK, NCAND])
        iota = sb("iota_sb", [P, NCAND])
        tot = sb("total", [P, PH])
        smp_e = sb("sample_expert", [TS, PH * PK], U32)
        smp_w = sb("sample_weight", [TS, PH * PK])
        U = sb("u_rows", [P, RING, D])
        V = sb("v_rows", [P, RING, D])
        atu = sb("u_rows_at", [P, 2, PK], U32)
        atv = sb("v_rows_at", [P, 2, PK], U32)
        dots = sb("dots", [P, 2, PK])
        gl = sb("gelu", [P, PK])
        wt = sb("expert_w", [P, 2, PK])
        dg = sb("diag", [P, DG, P])
        zero = sb("zero", [P, P])
        ai = sb("alpha_ident", [P, P])
        fold = sb("fold", [P, 2, TS])
        y = sb("y", [P, D])
        gain, offset = sb("ln2_g_sb", [P, D]), sb("ln2_b_sb", [P, D])
        st, mv = sb("ln2_st", [P, 12]), sb("ln2_mv", [P, 2])
        acc = ctx.enter_context(nc.psum_tensor("acc", [P, D], F32))
        pq = ctx.enter_context(nc.psum_tensor("pq_ps", [P, 2, 512], F32))
        pss = ctx.enter_context(nc.psum_tensor("key_ps", [P, 2, 512], F32))
        ident, h1, h1T = res["ident"], res["h1"], res["h1T"]
        expert, weight = sb("expert", [P, TILES, PH * PK], U32), sb("weight", [P, TILES, PH * PK])
        experts = expert[:].rearrange("p t k -> p (t k)")
        weights = weight[:].rearrange("p t k -> p (t k)")
        u_in = [sem(f"u_in{j}") for j in range(RING)]
        v_in = [sem(f"v_in{j}") for j in range(RING)]
        wq_in = [sem("w_pq_in0"), sem("w_pq_in1")]
        (pk_in, ln_in, q_ready, q_copied, s_ready, s_copied, top_done, step, hot_step, hot_done, e_asked, e_given, picked,
         at_set, pool_seen, dve_seen, dot_done, gelu_done, w_done, diag_done, v_used, sum_done, acc_read, y_step, y_ready, y_out,
         root_asked, root_given, const_set, spread) = (sem(n) for n in (
            "pk_in", "ln2_in", "pq_ready", "pq_copied", "key_ready", "key_copied", "top_done", "pick_step", "hot_step", "hot_done",
            "exp_asked", "exp_given", "picked", "at_set", "pool_seen", "dve_seen", "dot_done", "gelu_done", "w_done", "diag_done",
            "v_used", "sum_done", "acc_read", "y_step", "y_ready", "y_out", "root2_asked", "root2_given", "const_set", "spread"))
        head_picked = sem("head_picked")

        def group_tokens(g):
            a = GROUPS[g][0] * P
            return a, a + sum(ROWS[t] for t in GROUPS[g])

        def queries(g):
            return [("query", g, b) for b in range(NB + 1)]

        def pick(t):
            return [("pick", t, part) for part in range(PH + 2)]

        def spaced(items, n):
            return [items[len(items) * i // n:len(items) * (i + 1) // n] for i in range(n)]

        def extras(t):
            q1, q2 = queries(1), queries(2)
            steps = {0: pick(1)[0:1] + spread_over(pick(1)[1:], q1[0:8]), 1: q1[8:] + pick(2),
                     4: spread_over(pick(5), q2[0:8]), 5: q2[8:] + pick(6), SAMPLE: []}
            if t == 0:
                return [pick(0)[2:]] + spaced(steps[0], PH - 1)
            return spaced(steps[t], PH if t < SAMPLE else 2) if t in steps else None

        def spread_over(one, two):
            at = [((i + 0.5) / len(x), k, x[i]) for k, x in enumerate((one, two)) for i in range(len(x))]
            return [step for _, _, step in sorted(at, key=lambda v: v[:2])]

        def after_rows(steps):
            rows = [[] for _ in range(PK)]
            for i, s in enumerate(steps):
                rows[(i + 1) * PK // (len(steps) + 1) - 1].append(s)
            return rows
        ALONE = after_rows([])

        def turns(eng, side, turn, boundary, close=lambda n, b: None):
            for s in queries(0) + pick(0)[0:2]:
                side(s)
            for t in range(TILES):
                ex = extras(t)
                if ex is not None:
                    for h, steps in enumerate(ex):
                        turn(t * PH + h, h % 2, t, h, after_rows(steps))
                        close(t * PH + h, h % 2)
                        if h == 0 and t:
                            boundary(t - 1)
                    continue
                beside = {0: (0,), 1: (1, 2), 6: (7, 8, 9), 7: ()}
                for h in (0, 1, 6, 7):
                    if h == 6:
                        with eng.Fori(0, (PH - 4) // 2) as pair:
                            for x in range(2):
                                n = pair * 2 + (t * PH + 2 + x)
                                turn(n, x, t, None, ALONE)
                                side(("pick", t + 1, pair * 2 + (3 + x)))
                                close(n, x)
                    turn(t * PH + h, h % 2, t, h, ALONE)
                    for part in beside[h]:
                        side(("pick", t + 1, part))
                    close(t * PH + h, h % 2)
                    if h == 0:
                        boundary(t - 1)
            turn(MAIN * PH + 2, 0, None, 0, ALONE)
            boundary(SAMPLE)

        with nc.Block() as block:
            @block.sync
            def _(sp):
                wv = io["w_pq"].rearrange("(k p) n -> p k n", p=P)

                def load(i):
                    if i >= 2:
                        sp.wait_ge(q_ready, i - 1)
                    b = i % NB
                    sp.dma_start(wq[:, i % 2, :, :], wv[:, :, b * P:(b + 1) * P]).then_inc(wq_in[i % 2], 16)
                load(0)
                sp.dma_start(pk[:], io["pkT"]).then_inc(pk_in, 16)
                sp.dma_start(iota[:], io["iota"]).then_inc(pk_in, 16)
                load(1)
                for i in range(2, NB):
                    load(i)
                sp.dma_start(gain[:], io["ln2_g"].to_broadcast([P, D])).then_inc(ln_in, 16)
                sp.dma_start(offset[:], io["ln2_b"].to_broadcast([P, D])).then_inc(ln_in, 16)
                for i in range(NB, 2 * NB):
                    load(i)

                def store(t):
                    sp.wait_ge(y_ready, t + 1)
                    dst = io["y_p"][t * P:(t + 1) * P, :] if t < SAMPLE else io["y_s"]
                    sp.dma_start(dst, y[0:ROWS[t], :]).then_inc(y_out, 16)
                store(0)
                store(1)
                store(2)
                load(2 * NB)
                load(2 * NB + 1)
                store(3)
                for i in range(2 * NB + 2, 3 * NB):
                    load(i)
                for t in range(4, TILES):
                    store(t)
                sp.wait_ge(y_out, 16 * TILES)

            @block.gpsimd
            def _(pool):
                def hold(n):
                    if not isinstance(n, int):
                        pool.sem_inc(pool_seen, 1)

                def turn(n, b, t, h, steps):
                    first, last = isinstance(n, int) and n == 0, t is None
                    if t == 0:
                        pool.wait_ge(head_picked, h + 1)
                    elif h == 0 and not last:
                        pool.wait_ge(picked, t + 1)
                    if not last:
                        if not isinstance(n, int) or n >= 2:
                            pool.wait_ge(u_in[RING - 1], n * 32 - 32)
                        pool.tensor_copy(atu[:, b, :], experts[:, bass.ds(n * PK, PK)]).then_inc(at_set, 1)
                    if not first:
                        if not isinstance(n, int) or n >= 3:
                            pool.wait_ge(v_in[RING - 1], n * 32 - 64)
                        pool.tensor_copy(atv[:, b, :], experts[:, bass.ds(n * PK - PK, PK)]).then_inc(at_set, 1)
                    pool.wait_ge(at_set, n * 2 + (0 if last else 1))
                    hold(n)
                    for j in range(PK):
                        if not last:
                            if not isinstance(n, int) or n * PK + j >= RING:
                                pool.wait_ge(dot_done, n * PK + (j + 1 - RING))
                                hold(n)
                            pool.indirect_dma_start(out=U[:, j % RING, :], out_offset=None, in_=io["pu"],
                                                    in_offset=bass.IndirectOffsetOnAxis(ap=atu[:, b, j:j + 1], axis=0)).then_inc(u_in[j % RING], 16)
                        if not first:
                            if not isinstance(n, int) or (n - 1) * PK + j >= RING:
                                pool.wait_ge(v_used, n * PK + (j + 1 - RING - PK))
                                hold(n)
                            pool.indirect_dma_start(out=V[:, j % RING, :], out_offset=None, in_=io["pv"],
                                                    in_offset=bass.IndirectOffsetOnAxis(ap=atv[:, b, j:j + 1], axis=0)).then_inc(v_in[j % RING], 16)

                turns(pool, lambda s: None, turn, lambda t: None)

            @block.tensor
            def _(pe):
                pe.wait_ge(const_set, 5)
                pe.wait_ge(pk_in, 32)

                def side(s):
                    if s[0] != "query":
                        return
                    _, g, b = s
                    a, e = group_tokens(g)
                    i = g * NB + b
                    if b < NB:
                        pe.wait_ge(wq_in[i % 2], 16 * (i // 2 + 1))
                        if i >= 2:
                            pe.wait_ge(q_copied, i - 1)
                        for kk in range(KD):
                            last = pe.matmul(pq[:, i % 2, 0:e - a], wq[:, i % 2, kk, :], h1T[:, kk, a:e], start=(kk == 0), stop=(kk == KD - 1))
                        last.then_inc(q_ready, 1)
                    if b >= 1:
                        i -= 1
                        pe.wait_ge(q_copied, i + 1)
                        if i >= 2:
                            pe.wait_ge(s_copied, i - 1)
                        for x, t in enumerate(GROUPS[g]):
                            last = pe.matmul(pss[0:ROWS[t], i % 2, x * P:(x + 1) * P], qT[:, i % 2, x * P:x * P + ROWS[t]], pk[:, b - 1, :],
                                             start=True, stop=True)
                        last.then_inc(s_ready, 1)

                def turn(n, b, t, h, steps):
                    if isinstance(n, int) and n == 0:
                        for s in sum(steps, []):
                            side(s)
                        return
                    tile = (SAMPLE if t is None else t - 1 if h == 0 else t)
                    R = ROWS[tile]
                    if h == 1:
                        if tile:
                            pe.wait_ge(acc_read, tile)
                        w = ai[:] if R == P else fold[:, 1, :]
                        if tile == SAMPLE:
                            pe.wait_ge(spread, 2)
                        for c in range(2):
                            pe.matmul(acc[0:R, c * 512:(c + 1) * 512], w, h1[:, tile, c * 512:(c + 1) * 512], start=True, stop=False)
                    for j in range(PK):
                        pe.wait_ge(diag_done, n * PK + (j + 1 - PK))
                        pe.wait_ge(v_in[j % RING], n * 32 + (16 * (j // RING) + 16 - 32))
                        for c in range(2):
                            last = pe.matmul(acc[0:R, c * 512:(c + 1) * 512], dg[:, j % DG, 0:R], V[:, j % RING, c * 512:(c + 1) * 512],
                                             start=False, stop=False)
                        last.then_inc(v_used, 1)
                        for s in steps[j]:
                            side(s)
                    if h == 0:
                        for c in range(2):
                            last = pe.matmul(acc[0:R, c * 512:(c + 1) * 512], zero[:, 0:R], h1[:, tile, c * 512:(c + 1) * 512], start=False, stop=True)
                        last.then_inc(sum_done, 1)

                turns(pe, side, turn, lambda t: None)

            @block.scalar
            def _(act):
                def side(s):
                    if s[0] == "pick":
                        _, t, part = s
                        if isinstance(part, int) and part == PH + 1:
                            act.wait_ge(e_asked, t + 1)
                            act.activation(top[0:ROWS[t]], top[0:ROWS[t]], ACT.Exp).then_inc(e_given, 1)
                        return
                    _, g, b = s
                    a, e = group_tokens(g)
                    i = g * NB + b
                    if b < NB:
                        act.wait_ge(q_ready, i + 1)
                        if i >= 2:
                            act.wait_ge(s_ready, i - 1)
                        act.copy(qT[:, i % 2, 0:e - a], pq[:, i % 2, 0:e - a]).then_inc(q_copied, 1)
                    if b >= 1:
                        i -= 1
                        act.wait_ge(s_ready, i + 1)
                        if i >= 2:
                            act.wait_ge(top_done, i - 1)
                        full = sum(ROWS[t] == P for t in GROUPS[g])
                        last = act.copy(kw[:, i % 2, 0:full, :], pss[:, i % 2, 0:full * P].rearrange("p (x k) -> p x k", k=P))
                        if full < len(GROUPS[g]):
                            last = act.copy(kw[0:TS, i % 2, full, :], pss[0:TS, i % 2, full * P:(full + 1) * P])
                        last.then_inc(s_copied, 1)

                def turn(n, b, t, h, steps):
                    if not (isinstance(n, int) and n == 0):
                        tile = (SAMPLE if t is None else t - 1 if h == 0 else t)
                        src = ident[:] if tile < SAMPLE else fold[:, 0, :]
                        act.wait_ge(w_done, n)
                        for j in range(PK):
                            if not isinstance(n, int) or n > 1 or j >= DG:
                                act.wait_ge(v_used, n * PK + (j + 1 - DG - PK))
                            act.activation(dg[:, j % DG, 0:ROWS[tile]], src, ACT.Copy, scale=wt[:, 1 - b, j:j + 1]).then_inc(diag_done, 1)
                            for s in steps[j]:
                                side(s)
                    else:
                        for s in sum(steps, []):
                            side(s)
                    if t is not None:
                        act.wait_ge(dot_done, n * PK + PK)
                        if not isinstance(n, int) or n > 0:
                            act.wait_ge(w_done, n)
                        act.activation(gl[:, :], dots[:, b, :], ACT.Gelu).then_inc(gelu_done, 1)

                def boundary(t):
                    act.wait_ge(root_asked, t + 1)
                    act.activation(mv[0:ROWS[t], 1:2], mv[0:ROWS[t], 1:2], ACT.Sqrt).then_inc(root_given, 1)

                for q in range(1, P // TS):
                    last = act.copy(h1[q * TS:(q + 1) * TS, SAMPLE, :], h1[0:TS, SAMPLE, :])
                last.then_inc(spread, 2)
                act.wait_ge(const_set, 5)
                turns(act, side, turn, boundary)

            @block.vector
            def _(dve):
                cl = Link(dve, const_set)
                cl.add(dve.memset(zero[:], 0.0))
                cl.add(dve.tensor_scalar(ai[:], ident[:], ALPHA, None, ALU.mult))
                cl.add(dve.memset(fold[:, 1, :], 0.0))
                for q in range(P // TS):
                    last = dve.tensor_copy(fold[q * TS:(q + 1) * TS, 0, :], ident[q * TS:(q + 1) * TS, q * TS:(q + 1) * TS])
                cl.add(last)
                cl.wait()
                cl.add(dve.tensor_scalar(fold[0:TS, 1, :], ident[0:TS, 0:TS], ALPHA, None, ALU.mult))
                cl.wait()
                dve.wait_ge(pk_in, 32)
                link = Link(dve, step)

                def top16(values, at, work, n):
                    link.wait()
                    for lo in (0, 8):
                        for x in range(n):
                            link.add(dve.max(values(x)[:, lo:lo + 8], work(x)))
                        link.wait()
                        for x in range(n):
                            link.add(dve.max_index(at(x)[:, lo:lo + 8], values(x)[:, lo:lo + 8], work(x)))
                        link.wait()
                        if lo == 0:
                            for x in range(n):
                                link.add(dve.match_replace(work(x), values(x)[:, 0:8], work(x), GONE))
                            link.wait()

                def candidates(t):
                    R, s = ROWS[t], t % 4
                    link.wait()
                    link.add(dve.tensor_copy(fi[0:R], iu[0:R, s]))
                    link.wait()
                    i1 = fi[0:R].rearrange("p (h two) k -> p h two k", two=2)
                    vv = v[0:R, s].rearrange("p (h two) k -> p h two k", two=2)
                    link.add(dve.tensor_scalar(i1[:, :, 0, :], i1[:, :, 0, :], float(NKEYS), None, ALU.mult))
                    link.wait()
                    for src, dst in ((vv, cand), (i1, cidx)):
                        for i, m, n, o in stair_runs():
                            for x in range(m) if n > 1 else (0,):
                                if n > 1:
                                    out = dst[0:R, :, o + x * n:o + (x + 1) * n]
                                    one = src[:, :, 0, i + x:i + x + 1].to_broadcast([R, PH, n])
                                    two = src[:, :, 1, 0:n]
                                else:
                                    out = dst[0:R, :, o:o + m]
                                    one = src[:, :, 0, i:i + m]
                                    two = src[:, :, 1, 0:1].to_broadcast([R, PH, m])
                                link.add(dve.tensor_tensor(out, one, two, ALU.add))
                    link.wait()
                    top16(lambda x: top[0:R, x, :], lambda x: tat[0:R, x, :], lambda x: cand[0:R, x, :], PH)
                    link.add(dve.tensor_copy(taf[0:R], tat[0:R]))
                    link.wait()

                def side(s):
                    if s[0] == "query":
                        _, g, b = s
                        if b == 0:
                            return
                        i = g * NB + b - 1
                        dve.wait_ge(s_copied, i + 1)
                        for rows in ([x for x, t in enumerate(GROUPS[g]) if ROWS[t] == P], [x for x, t in enumerate(GROUPS[g]) if ROWS[t] < P]):
                            if rows:
                                R = ROWS[GROUPS[g][rows[0]]]
                                at = [GROUPS[g][x] % 4 for x in rows]
                                top16(lambda x: v[0:R, at[x], b - 1, :], lambda x: iu[0:R, at[x], b - 1, :],
                                      lambda x: kw[0:R, i % 2, rows[x], :], len(rows))
                        dve.sem_inc(top_done, 1)
                        return
                    _, t, part = s
                    R = ROWS[t]
                    if isinstance(part, int) and part == 0:
                        return candidates(t)
                    if isinstance(part, int) and part == PH + 1:
                        dve.wait_ge(hot_done, PH * (t + 1))
                        e_to, w_to = (expert[:, t, :], weight[:, t, :]) if t < SAMPLE else (smp_e, smp_w)
                        if t:
                            link.add(dve.tensor_copy(e_to[0:R, :].rearrange("p (h k) -> p h k", k=PK), ef[0:R]))
                        link.add(dve.tensor_copy(tot[0:R, :].unsqueeze(2), top[0:R, :, 0:1]))
                        link.wait()
                        dve.tensor_tensor(top[0:R], top[0:R], tot[0:R, :].unsqueeze(2).to_broadcast([R, PH, PK]), ALU.subtract).then_inc(e_asked, 1)
                        dve.wait_ge(e_given, t + 1)
                        link.add(dve.tensor_reduce(tot[0:R, :], top[0:R], AX.X, ALU.add))
                        link.wait()
                        link.add(dve.reciprocal(tot[0:R, :], tot[0:R, :]))
                        link.wait()
                        ins = dve.tensor_tensor(w_to[0:R, :].rearrange("p (h k) -> p h k", k=PK), top[0:R],
                                                tot[0:R, :].unsqueeze(2).to_broadcast([R, PH, PK]), ALU.mult)
                        if t < SAMPLE:
                            ins.then_inc(picked, 1)
                            dve.wait_ge(picked, t + 1)
                            return
                        link.add(ins)
                        link.wait()
                        for q in range(P // TS):
                            dve.tensor_copy(weight[q * TS:(q + 1) * TS, SAMPLE, 0:NS], smp_w[:, q * NS:(q + 1) * NS])
                            last = dve.tensor_copy(expert[q * TS:(q + 1) * TS, SAMPLE, 0:NS], smp_e[:, q * NS:(q + 1) * NS])
                        last.then_inc(picked, 1)
                        dve.wait_ge(picked, t + 1)
                        return
                    hh, c = part - 1, part + (PH * t - 1)
                    if isinstance(part, int):
                        row = slice(hh, hh + 1)
                    else:
                        row = bass.ds(hh, 1)
                    dve.wait_ge(hot_done, c) if not isinstance(c, int) or c > 0 else None
                    dve.tensor_tensor(hot[0:R], iota[0:R, :].unsqueeze(1).to_broadcast([R, PK, NCAND]),
                                      taf[0:R, row, :].rearrange("p o k -> p (o k)").unsqueeze(2).to_broadcast([R, PK, NCAND]),
                                      ALU.is_equal).then_inc(hot_step, 1)
                    dve.wait_ge(hot_step, c * 2 + 1)
                    dve.tensor_tensor(hot[0:R], hot[0:R], cidx[0:R, row, :].to_broadcast([R, PK, NCAND]), ALU.mult).then_inc(hot_step, 1)
                    dve.wait_ge(hot_step, c * 2 + 2)
                    dve.tensor_reduce(ef[0:R, row, :].rearrange("p o k -> p (o k)"), hot[0:R], AX.X, ALU.add).then_inc(hot_done, 1)
                    if t == 0:
                        dve.wait_ge(hot_done, part)
                        dve.tensor_copy(expert[:, 0, hh * PK:(hh + 1) * PK], ef[:, hh, :]).then_inc(head_picked, 1)

                def turn(n, b, t, h, steps):
                    if t is None:
                        return
                    if t == SAMPLE and h == 0:
                        dve.wait_ge(spread, 2)
                    for j in range(PK):
                        dve.wait_ge(u_in[j % RING], n * 32 + (16 * (j // RING) + 16))
                        dve.tensor_tensor_reduce(U[:, j % RING, :], U[:, j % RING, :], h1[:, t, :], 1.0, 0.0, ALU.mult, ALU.add,
                                                 dots[:, b, j:j + 1]).then_inc(dot_done, 1)
                        for s in steps[j]:
                            side(s)

                def close(n, b):
                    dve.wait_ge(gelu_done, n + 1)
                    dve.tensor_tensor(wt[:, b, :], gl[:, :], weights[:, bass.ds(n * PK, PK)], ALU.mult).then_inc(w_done, 1)

                def boundary(t):
                    R = ROWS[t]
                    if t == 0:
                        dve.wait_ge(ln_in, 32)
                    dve.wait_ge(sum_done, t + 1)
                    if t:
                        dve.wait_ge(y_out, t * 16)
                        dve.wait_ge(y_ready, t)
                    x = y[0:R, :]
                    dve.tensor_copy(x, acc[0:R, :]).then_inc(acc_read, 1)
                    dve.wait_ge(acc_read, t + 1)
                    layer_norm(dve, yl, x, st, mv, gain, offset, R, root_asked, root_given, t).then_inc(y_ready, 1)
                yl = Link(dve, y_step)
                turns(dve, side, turn, boundary, close)


def streaming_step(nc, io):
    with ExitStack() as ctx:
        def sb(name, shape, dt=F32):
            return ctx.enter_context(nc.sbuf_tensor(name, shape, dt))

        def sem(name):
            return ctx.enter_context(nc.semaphore(name))
        res = {"ident": sb("ident_sb", [P, P]), "xT": sb("xT_sb", [P, KD, NT]), "late": sb("late", [P, TILES * D])}
        res["oaT"] = res["late"][:, 0:4 * NT].rearrange("p (k n) -> p k n", k=4)
        res["obT"] = res["late"][:, 4 * NT:8 * NT].rearrange("p (k n) -> p k n", k=4)
        res["h1"] = res["late"][:].rearrange("p (t d) -> p t d", t=TILES)
        res["h1T"] = res["xT"]
        res["tail"] = res["late"][:, 8 * NT:TILES * D]
        gated_linear(nc, io, res, sem)
        mixed = ctx.enter_context(ExitStack())
        res["mT"] = mixed.enter_context(nc.sbuf_tensor("mT", [P, KD, NT], F32))
        with ExitStack() as att:
            def own(name, shape):
                return att.enter_context(nc.sbuf_tensor(name, shape, F32))
            res |= {"aqT": own("aqT", [P, GROUP, NT]), "iqT": own("iqT", [P, 2, NT]), "iw": own("iw", [P, TILES, IH]),
                    "kT": own("kT", [P, TP]), "ikT": own("ikT", [P, TP]), "V": own("V", [P, TP // P, P]),
                    "kTs": own("kTs", [P, PAST + TS]), "ikTs": own("ikTs", [P, PAST + TS]), "Vs": own("Vs", [P, PAST // P + 1, P])}
            project_attention(nc, io, res, sem)
            sparse_attention(nc, io, res, sem)
        merge(nc, io, res, sem)
        mixed.close()
        run_experts(nc, io, res, sem)


def constants(np):
    half = HD // 2
    inv = np.float32(10000.0) ** (-np.arange(half, dtype=np.float32) / np.float32(half))
    pos = np.concatenate([np.arange(TP), PAST + np.arange(TS)]).astype(np.float32)
    ang = (pos[:, None] * inv[None, :]).astype(np.float32)

    def tiles(a):
        out = np.zeros((P, TILES, a.shape[1]), np.float32)
        for t in range(TILES):
            out[:ROWS[t], t] = a[t * P:t * P + ROWS[t]]
        return out
    cos, sin = np.cos(ang), np.sin(ang)
    s, t = np.arange(P)[:, None], np.arange(P)[None, :]
    reset = np.ones((P, NT), np.float32)
    reset[:, ::GC] = 0.0
    return {
        "ident": np.eye(P, dtype=np.float32),
        "cos": tiles(np.concatenate([cos, cos], 1)), "sin": tiles(np.concatenate([-sin, sin], 1)),
        "gla_mask": ((s <= t) & (s // GC == t // GC)).astype(np.float32), "reset": reset,
        "iota": np.tile(np.arange(NCAND, dtype=np.float32), (P, 1)),
    }


OUTS = {"y_p": (TP, D), "y_s": (TS, D), "k_p": (TP, KV * HD), "v_p": (TP, KV * HD), "ik_p": (TP, ID),
        "gla_p": (GH, GK, GK), "k_s": (TS, KV * HD), "v_s": (TS, KV * HD), "ik_s": (TS, ID), "gla_s": (GH, GK, GK)}


def layouts(np, v):
    x = np.concatenate([v["x_prompt"][0], v["x_sample"][0]], 0)
    keys = np.stack([v["pk1"][0], v["pk2"][0]], 1).reshape(2 * PH, NKEYS, P)
    ik = v["cache_idx_k"][0, 0].T
    return {
        "xT": x.T.reshape(KD, P, NT).transpose(1, 0, 2), "x_p": v["x_prompt"][0], "x_s": v["x_sample"][0],
        "kcT": v["cache_k"][0, 0].reshape(PAST, KV * HD).T, "ikcT": np.concatenate([ik, ik], 0),
        "vc": v["cache_v"][0, 0].reshape(PAST, KV * HD), "state": v["state_gla"][0, 0],
        "w_in": v["w_in"][0], "w_fa": v["w_fa"][0], "b_fa": v["b_fa"][0].reshape(GH, GK).T, "g_gla_norm": v["g_gla_norm"],
        "w_pa": v["w_pa"][0], "w_pb": v["w_pb"][0], "w_out": v["w_out"][0], "w_pq": v["w_pq"][0],
        "pkT": keys.transpose(2, 0, 1), "pu": v["pu"][0], "pv": v["pv"][0],
        "ln1_g": v["ln1_g"], "ln1_b": v["ln1_b"], "ln2_g": v["ln2_g"], "ln2_b": v["ln2_b"],
    }


def kernel(**inputs):
    import numpy as np
    import concourse.bacc as bacc
    from concourse.bass_utils import run_bass_kernel_spmd

    arrays = {n: np.ascontiguousarray(a) for n, a in (layouts(np, inputs) | constants(np)).items()}
    nc = bacc.Bacc("TRN2", target_bir_lowering=False, num_devices=1)
    io = {n: nc.dram_tensor(f"in_{n}", a.shape, F32, kind="ExternalInput").ap() for n, a in arrays.items()}
    io |= {n: nc.dram_tensor(f"out_{n}", s, F32, kind="ExternalOutput").ap() for n, s in OUTS.items()}
    streaming_step(nc, io)
    r = run_bass_kernel_spmd(nc, [{f"in_{n}": a for n, a in arrays.items()}], core_ids=[0]).results[0]
    o = {n: r[f"out_{n}"] for n in OUTS}
    return (o["y_p"].reshape(1, TP, D), o["y_s"].reshape(1, TS, D),
            o["k_p"].reshape(1, 1, TP, KV, HD), o["v_p"].reshape(1, 1, TP, KV, HD), o["ik_p"].reshape(1, 1, TP, ID),
            o["gla_p"].reshape(1, 1, GH, GK, GK),
            o["k_s"].reshape(1, 1, TS, KV, HD), o["v_s"].reshape(1, 1, TS, KV, HD), o["ik_s"].reshape(1, 1, TS, ID),
            o["gla_s"].reshape(1, 1, GH, GK, GK))
```
